# Optimizing a Trainium2 kernel written in Bass

```python
import jax, jax.numpy as jnp
from jax import lax
import numpy as np

D_MODEL = 2048
BATCH = 1
SEQ = 256
DEPTH = 1

CHUNK = 64
H_A = 8
DK_A = 128
DV_A = 128
D_A = H_A * DK_A
H_B = 8
DH_B = 128
D_B = H_B * DH_B
N_PAST_CHUNKS = 8
BAND = N_PAST_CHUNKS + 1
REL_FUTURE = CHUNK - 1
REL_PAST = 2 * CHUNK - 1
N_REL = REL_FUTURE + REL_PAST + 1
D_FF = -(-8 * D_MODEL // (3 * 256)) * 256
N_IN = 4 * D_A + 3 * D_B + 2 * D_MODEL
EPS = 1e-6


def rms_norm(x, gain):
    xf = x.astype(jnp.float32)
    y = xf * lax.rsqrt(jnp.mean(xf * xf, axis=-1, keepdims=True) + EPS)
    return (y * gain.astype(jnp.float32)).astype(x.dtype)

def hgrn_lower_bounds(lb_logits):
    p = jax.nn.softmax(lb_logits.astype(jnp.float32), axis=0)
    return jnp.cumsum(p, axis=0)[:DEPTH]

def hgrn2_mixer(q, f_logit, i, g, lb, out_gain):
    B, T, _ = q.shape
    n_chunks = T // CHUNK
    f32 = jnp.float32
    lbf = lb.astype(f32)
    f = lbf + (1.0 - lbf) * jax.nn.sigmoid(f_logit.astype(f32))
    log_f = jnp.log(f)
    k = 1.0 - f
    qs = jax.nn.silu(q.astype(f32))

    def to_chunks(t, dh):
        return t.reshape(B, n_chunks, CHUNK, H_A, dh).transpose(1, 0, 3, 2, 4)

    qc, kc, lfc = to_chunks(qs, DK_A), to_chunks(k, DK_A), to_chunks(log_f, DK_A)
    vc = to_chunks(i.astype(f32), DV_A)
    causal = jnp.tril(jnp.ones((CHUNK, CHUNK), dtype=bool))[:, :, None]

    def step(S, inp):
        qj, kj, lfj, vj = inp
        b = jnp.cumsum(lfj, axis=2)
        o_inter = jnp.einsum('bhtk,bhkv->bhtv', qj * jnp.exp(b), S)
        rel = jnp.where(causal, b[:, :, :, None, :] - b[:, :, None, :, :], -jnp.inf)
        decay = jnp.exp(rel)
        scores = jnp.einsum('bhtk,bhsk,bhtsk->bhts', qj, kj, decay)
        o_intra = jnp.einsum('bhts,bhsv->bhtv', scores, vj)
        b_last = b[:, :, -1:, :]
        S_new = jnp.exp(b_last[:, :, 0, :, None]) * S + jnp.einsum(
            'bhsk,bhsv->bhkv', kj * jnp.exp(b_last - b), vj)
        return S_new, o_inter + o_intra

    S0 = jnp.zeros((B, H_A, DK_A, DV_A), f32)
    _, o = lax.scan(step, S0, (qc, kc, lfc, vc))
    o = o.transpose(1, 0, 3, 2, 4).reshape(B, T, H_A, DV_A)
    o = o * lax.rsqrt(jnp.mean(o * o, axis=-1, keepdims=True) + EPS)
    o = o.reshape(B, T, D_A) * out_gain.astype(f32)
    o = o * jax.nn.silu(g.astype(f32))
    return o.astype(q.dtype)

def head_rms_norm(t, gain):
    tf = t.astype(jnp.float32)
    y = tf * lax.rsqrt(jnp.mean(tf * tf, axis=-1, keepdims=True) + EPS)
    return y * gain.astype(jnp.float32)

def chunked_relpos_attention(q, k, v, q_gain, k_gain, rel_bias):
    B, T, _ = q.shape
    n_chunks = T // CHUNK

    def heads(t):
        return t.reshape(B, n_chunks, CHUNK, H_B, DH_B).transpose(0, 3, 1, 2, 4)

    qh = head_rms_norm(heads(q), q_gain)
    kh = head_rms_norm(heads(k), k_gain)
    vh = heads(v).astype(jnp.float32)

    pad = ((0, 0), (0, 0), (N_PAST_CHUNKS, 0), (0, 0), (0, 0))
    band_idx = jnp.arange(n_chunks)[:, None] + jnp.arange(BAND)[None, :]
    k_band = jnp.pad(kh, pad)[:, :, band_idx].reshape(B, H_B, n_chunks, BAND * CHUNK, DH_B)
    v_band = jnp.pad(vh, pad)[:, :, band_idx].reshape(B, H_B, n_chunks, BAND * CHUNK, DH_B)

    q_pos = jnp.arange(n_chunks)[:, None] * CHUNK + jnp.arange(CHUNK)[None, :]
    k_chunk = band_idx - N_PAST_CHUNKS
    k_pos = (k_chunk[:, :, None] * CHUNK + jnp.arange(CHUNK)[None, None, :]).reshape(
        n_chunks, BAND * CHUNK)
    valid = k_pos >= 0
    dist = q_pos[:, :, None] - k_pos[:, None, :]
    rel_idx = jnp.clip(dist, -REL_FUTURE, REL_PAST) + REL_FUTURE
    bias = rel_bias.astype(jnp.float32)[:, rel_idx]

    scale = DH_B ** -0.5
    scores = jnp.einsum('bhnqd,bhnkd->bhnqk', qh, k_band) * scale + bias[None]
    scores = jnp.where(valid[None, None, :, None, :], scores, -jnp.inf)
    p = jax.nn.softmax(scores, axis=-1)
    o = jnp.einsum('bhnqk,bhnkd->bhnqd', p, v_band)
    return o.transpose(0, 2, 3, 1, 4).reshape(B, T, D_B).astype(q.dtype)

def first_inputs(seed: int = 0) -> dict:
    key = jax.random.key(seed)
    ks = jax.random.split(key, 16)
    f32 = jnp.float32

    def nrm(k, shape, scale):
        return jax.random.normal(k, shape, f32) * scale

    return {
        "x": nrm(ks[0], (BATCH, SEQ, D_MODEL), 1.0),
        "w_in": nrm(ks[1], (DEPTH, D_MODEL, N_IN), D_MODEL ** -0.5),
        "b_gate": nrm(ks[2], (DEPTH, 2 * D_MODEL), 0.02),
        "norm_mix": 1.0 + nrm(ks[3], (DEPTH, D_MODEL), 0.02),
        "norm_ffn": 1.0 + nrm(ks[4], (DEPTH, D_MODEL), 0.02),
        "hgrn_lb_logits": nrm(ks[5], (DEPTH + 1, D_A), 0.5),
        "hgrn_out_gain": 1.0 + nrm(ks[6], (DEPTH, D_A), 0.02),
        "q_gain": 1.0 + nrm(ks[7], (DEPTH, DH_B), 0.02),
        "k_gain": 1.0 + nrm(ks[8], (DEPTH, DH_B), 0.02),
        "rel_bias": nrm(ks[9], (DEPTH, H_B, N_REL), 0.1),
        "w_proj_a": nrm(ks[10], (DEPTH, D_A, D_MODEL), D_A ** -0.5),
        "w_proj_b": nrm(ks[11], (DEPTH, D_B, D_MODEL), D_B ** -0.5),
        "w_out": nrm(ks[12], (DEPTH, D_MODEL, D_MODEL), D_MODEL ** -0.5),
        "w_ffn_in": nrm(ks[13], (DEPTH, D_MODEL, 2 * D_FF), D_MODEL ** -0.5),
        "w_ffn_out": nrm(ks[14], (DEPTH, D_FF, D_MODEL), D_FF ** -0.5),
    }

def first_block(x, w_in, b_gate, norm_mix, norm_ffn, hgrn_lb_logits, hgrn_out_gain,
              q_gain, k_gain, rel_bias, w_proj_a, w_proj_b, w_out, w_ffn_in, w_ffn_out):
    lower_bounds = hgrn_lower_bounds(hgrn_lb_logits)
    split_pts = [D_A, 2 * D_A, 3 * D_A, 4 * D_A,
                 4 * D_A + D_B, 4 * D_A + 2 * D_B, 4 * D_A + 3 * D_B]
    for l in range(DEPTH):
        h = rms_norm(x, norm_mix[l])
        proj = jnp.einsum('btd,dn->btn', h, w_in[l])
        q_a, f_a, i_a, g_a, q_b, k_b, v_b, gate_logits = jnp.split(proj, split_pts, axis=-1)
        gates = jax.nn.sigmoid((gate_logits + b_gate[l]).astype(jnp.float32)).astype(x.dtype)
        gate_a, gate_b = jnp.split(gates, 2, axis=-1)

        y_a = hgrn2_mixer(q_a, f_a, i_a, g_a, lower_bounds[l], hgrn_out_gain[l])
        y_b = chunked_relpos_attention(q_b, k_b, v_b, q_gain[l], k_gain[l], rel_bias[l])

        merged = (gate_a * jnp.einsum('btc,cd->btd', y_a, w_proj_a[l])
                  + gate_b * jnp.einsum('btc,cd->btd', y_b, w_proj_b[l]))
        x = x + jnp.einsum('btd,de->bte', merged, w_out[l])

        h = rms_norm(x, norm_ffn[l])
        gate_up = jnp.einsum('btd,df->btf', h, w_ffn_in[l])
        ff_gate, ff_up = jnp.split(gate_up, 2, axis=-1)
        x = x + jnp.einsum('btf,fd->btd', jax.nn.silu(ff_gate) * ff_up, w_ffn_out[l])
    return x


N_MIXERS = 3
EXPAND = 2
D_INNER = EXPAND * D_MODEL
CHUNK_2 = 128
A_GROUPS = 8
A_GROUP_DIM = D_INNER // A_GROUPS
B_GROUPS = 8
B_GROUP_DIM = D_INNER // B_GROUPS
POOL_WINDOWS = (2, 4, 8, 16)
C_GROUPS = len(POOL_WINDOWS)
C_GROUP_DIM = D_INNER // C_GROUPS


def _layers_of_kind(kind):
    return len(range(kind, DEPTH, N_MIXERS))

def rmsnorm(x, g):
    xf = x.astype(jnp.float32)
    y = xf * lax.rsqrt(jnp.mean(xf * xf, axis=-1, keepdims=True) + EPS)
    return (y * g.astype(jnp.float32)).astype(x.dtype)

def gmlp_mixer(h, w_in, v_gain, w_s, b_s):
    bsz, seq, _ = h.shape
    z = h @ w_in
    u, v, gate = jnp.split(z, 3, axis=-1)
    u = jax.nn.gelu(u)
    v = rmsnorm(jax.nn.gelu(v), v_gain)
    vc = v.reshape(bsz, seq // CHUNK_2, CHUNK_2, A_GROUPS, A_GROUP_DIM)
    sv = jnp.einsum('gpq,bnqgc->bnpgc', w_s, vc) + b_s.T[None, None, :, :, None]
    y = u * sv.reshape(bsz, seq, D_INNER)
    return y, gate

def fourier_mixer(h, w_in, w_mix):
    bsz, seq, _ = h.shape
    z = h @ w_in
    xb, gate = jnp.split(z, 2, axis=-1)
    xg = xb.reshape(bsz, seq, B_GROUPS, B_GROUP_DIM).astype(jnp.float32)
    f = jnp.fft.fft2(xg, axes=(1, 3), norm="ortho").real.astype(xb.dtype)
    y = jnp.einsum('bsgc,gcd->bsgd', f, w_mix).reshape(bsz, seq, D_INNER)
    return y, gate

def pool_mixer(h, w_in, w_mix, scale):
    bsz, seq, _ = h.shape
    z = h @ w_in
    xc, gate = jnp.split(z, 2, axis=-1)
    xg = xc.reshape(bsz, seq, C_GROUPS, C_GROUP_DIM)
    t = jnp.arange(seq)
    pooled = []
    for gi, w in enumerate(POOL_WINDOWS):
        xi = xg[:, :, gi, :].astype(jnp.float32)
        csum = jnp.pad(lax.cumsum(xi, axis=1), ((0, 0), (1, 0), (0, 0)))
        lo = jnp.clip(t - w // 2, 0, seq - 1)
        hi = jnp.clip(t + w - 1 - w // 2, 0, seq - 1)
        wsum = jnp.take(csum, hi + 1, axis=1) - jnp.take(csum, lo, axis=1)
        cnt = (hi - lo + 1).astype(jnp.float32)[None, :, None]
        pooled.append(wsum / cnt - xi)
    p = jnp.stack(pooled, axis=2).astype(xc.dtype)
    y = jnp.einsum('bsgc,gcd->bsgd', p, w_mix).reshape(bsz, seq, D_INNER) * scale
    return y, gate

def second_inputs(seed: int = 0) -> dict:
    key = jax.random.key(seed)
    ks = jax.random.split(key, 20)
    na, nb, nc = _layers_of_kind(0), _layers_of_kind(1), _layers_of_kind(2)
    f32 = jnp.float32
    nrm = lambda k, shape, s: jax.random.normal(k, shape, f32) * s
    din = D_MODEL ** -0.5
    dout = D_INNER ** -0.5
    return {
        "x": jax.random.normal(ks[0], (BATCH, SEQ, D_MODEL), f32),
        "a_norm": 1.0 + nrm(ks[1], (na, D_MODEL), 0.05),
        "a_w_in": nrm(ks[2], (na, D_MODEL, 3 * D_INNER), din),
        "a_v_gain": 1.0 + nrm(ks[3], (na, D_INNER), 0.05),
        "a_w_s": nrm(ks[4], (na, A_GROUPS, CHUNK_2, CHUNK_2), 0.5 * CHUNK_2 ** -0.5),
        "a_b_s": 1.0 + nrm(ks[5], (na, A_GROUPS, CHUNK_2), 0.1),
        "a_w_out": nrm(ks[6], (na, D_INNER, D_MODEL), dout),
        "b_norm": 1.0 + nrm(ks[7], (nb, D_MODEL), 0.05),
        "b_w_in": nrm(ks[8], (nb, D_MODEL, 2 * D_INNER), din),
        "b_w_mix": nrm(ks[9], (nb, B_GROUPS, B_GROUP_DIM, B_GROUP_DIM), B_GROUP_DIM ** -0.5),
        "b_w_out": nrm(ks[10], (nb, D_INNER, D_MODEL), dout),
        "c_norm": 1.0 + nrm(ks[11], (nc, D_MODEL), 0.05),
        "c_w_in": nrm(ks[12], (nc, D_MODEL, 2 * D_INNER), din),
        "c_w_mix": nrm(ks[13], (nc, C_GROUPS, C_GROUP_DIM, C_GROUP_DIM), C_GROUP_DIM ** -0.5),
        "c_scale": 1.0 + nrm(ks[14], (nc, D_INNER), 0.1),
        "c_w_out": nrm(ks[15], (nc, D_INNER, D_MODEL), dout),
        "final_norm": 1.0 + nrm(ks[16], (D_MODEL,), 0.05),
    }

def second_block(x, a_norm, a_w_in, a_v_gain, a_w_s, a_b_s, a_w_out,
              b_norm, b_w_in, b_w_mix, b_w_out,
              c_norm, c_w_in, c_w_mix, c_scale, c_w_out, final_norm):
    for i in range(DEPTH):
        kind, j = i % N_MIXERS, i // N_MIXERS
        if kind == 0:
            h = rmsnorm(x, a_norm[j])
            y, gate = gmlp_mixer(h, a_w_in[j], a_v_gain[j], a_w_s[j], a_b_s[j])
            w_out = a_w_out[j]
        elif kind == 1:
            h = rmsnorm(x, b_norm[j])
            y, gate = fourier_mixer(h, b_w_in[j], b_w_mix[j])
            w_out = b_w_out[j]
        else:
            h = rmsnorm(x, c_norm[j])
            y, gate = pool_mixer(h, c_w_in[j], c_w_mix[j], c_scale[j])
            w_out = c_w_out[j]
        x = x + (y * jax.nn.silu(gate)) @ w_out
    return rmsnorm(x, final_norm)


def setup_inputs(seed=0):
    out = dict(first_inputs(seed))
    for name, value in second_inputs(seed + 1).items():
        if name != "x":
            out[name + "_2"] = value
    return out


def reference(
    x, w_in, b_gate, norm_mix, norm_ffn, hgrn_lb_logits, hgrn_out_gain, q_gain, k_gain,
    rel_bias, w_proj_a, w_proj_b, w_out, w_ffn_in, w_ffn_out, a_norm_2, a_w_in_2, a_v_gain_2,
    a_w_s_2, a_b_s_2, a_w_out_2, b_norm_2, b_w_in_2, b_w_mix_2, b_w_out_2, c_norm_2, c_w_in_2,
    c_w_mix_2, c_scale_2, c_w_out_2, final_norm_2,
):
    x = first_block(
        x, w_in, b_gate, norm_mix, norm_ffn, hgrn_lb_logits, hgrn_out_gain, q_gain, k_gain,
        rel_bias, w_proj_a, w_proj_b, w_out, w_ffn_in, w_ffn_out,
    )
    return second_block(
        x, a_norm_2, a_w_in_2, a_v_gain_2, a_w_s_2, a_b_s_2, a_w_out_2, b_norm_2, b_w_in_2,
        b_w_mix_2, b_w_out_2, c_norm_2, c_w_in_2, c_w_mix_2, c_scale_2, c_w_out_2, final_norm_2,
    )


_drawn_inputs = setup_inputs


def setup_inputs(seed=0):
    import zlib

    import numpy as np

    out = dict(_drawn_inputs(seed))
    spreads = {}
    factors = {'b_gate': 8.0,
     'norm_mix': 5.113,
     'norm_ffn': 15.246,
     'hgrn_lb_logits': 2.679,
     'hgrn_out_gain': 7.382,
     'q_gain': 8.0,
     'k_gain': 8.0,
     'rel_bias': 22.373,
     'a_v_gain_2': 59.624,
     'a_norm_2': 8.0,
     'a_b_s_2': 8.0}
    for name, (base, spread) in spreads.items():
        noise = np.random.default_rng([zlib.crc32(name.encode()), seed]).standard_normal(out[name].shape)
        drawn = base * np.exp(spread * noise) if base else spread * noise
        out[name] = __import__('jax').numpy.asarray(drawn.astype(out[name].dtype))
    for name, factor in factors.items():
        out[name] = (out[name] * factor).astype(out[name].dtype)
    return out
```

```python
from contextlib import ExitStack

import concourse.bass as bass
from concourse import mybir

ALU = mybir.AluOpType
ACT = mybir.ActivationFunctionType
F32 = mybir.dt.float32
F32R = mybir.dt.float32r
AX_X = mybir.AxisListType.X

P = 128
T = 256
TB = T // P
D = 2048
DT = D // P
H = 8
DH = 128
DM = H * DH
CHUNK = 64
N_REL = 191
REL_FUTURE = CHUNK - 1
FF = 5632
FT = FF // P
E2 = 4096
ET = E2 // P
G = 8
EPS = 1e-6
NEG = -3.0e38
LN_MIN = 2.0 ** -64

NB = 512
UK = 2
RING = 4
LEVELS = 8
MASKED = 7
EXT = 384


class Segment:

    def __init__(self, weights, form, steps, rows, first, stride, operand, tile0=0):
        self.w, self.form, self.steps, self.units = weights, form, steps, rows // (UK * P)
        self.first, self.stride = first, stride
        self.operand, self.tile0 = operand, tile0
        self.pair = 2 * self.units
        assert self.pair % RING == 0


class Chain:

    def __init__(self, eng, sem):
        self.eng, self.sem, self.base, self.step, self.at = eng, sem, 0, 0, 0

    def value(self):
        return self.at + self.base if not self.step else self.step[0] * self.step[1] + (self.base + self.at)

    def link(self, instruction):
        instruction.then_inc(self.sem, 1)
        self.at += 1
        self.eng.wait_ge(self.sem, self.value())

    def enter(self, i, per):
        self.base, self.at, self.step = self.base + self.at, 0, (i, per)

    def leave(self, steps):
        assert self.at == self.step[1], (self.at, self.step[1])
        self.base, self.at, self.step = self.base + steps * self.step[1], 0, 0


def build(nc, x, w_in, b_gate, norm_mix, norm_ffn, lb_logits, out_gain, q_gain, k_gain, rel_bias,
          w_proj_a, w_proj_b, w_out, w_ffn_in, w_ffn_out, a_norm, a_w_in, a_v_gain, a_w_s, a_b_s,
          a_w_out, final_norm, out):
    ctx = ExitStack()
    with ctx:
        top = [(nc.sbuf_base + 63) // 64 * 64]

        def at(name, shape, offset, dt=F32):
            return nc.alloc_sbuf_tensor_at(name, [P] + shape, dt, offset=offset)

        def size(shape):
            n = 4
            for s in shape:
                n *= s
            return n

        def new(name, shape, dt=F32):
            offset = top[0]
            top[0] += (size(shape) + 31) // 32 * 32
            return at(name, shape, offset, dt)

        raw = new("raw", [RING, UK, NB])
        w_hi = new("w_hi", [RING, UK, NB], F32R)
        w_lo = new("w_lo", [RING, UK, NB], F32R)
        a_at = top[0]
        a_hi = new("a_hi", [DT, T], F32R)
        a_lo = new("a_lo", [DT, T], F32R)
        x_t = new("x_t", [DT, T])
        x_fin = at("x_fin", [TB, D], a_at)
        gain_fin = at("gain_fin", [D], a_at + size([TB, D]))

        shared = top[0]
        top[0] += 88 * 1024
        KB = 1024
        qf = at("qf", [2 * H, T], shared)
        q_a = qf[:, 0:H]
        f_a = qf[:, H:2 * H]
        g_a = at("g_a", [3, H, T], shared + 16 * KB)
        q_b, k_b = g_a[:, 1], g_a[:, 2]
        val = at("val", [2, TB, DM], shared + 40 * KB)
        gates = at("gates", [2 * DT, T], shared + 56 * KB)
        x_tok = at("x_tok", [TB, D], shared + 56 * KB)
        keys = at("keys", [H, T], shared + 72 * KB)
        masks = at("masks", [MASKED, P], shared + 80 * KB)
        masked = at("masked", [MASKED, P], shared + 80 * KB + size([MASKED, P]))
        ff_hi = at("ff_hi", [FT, T], shared, F32R)
        ff_lo = at("ff_lo", [FT, T], shared + 44 * KB, F32R)
        v_g = at("v_g", [G, TB, NB], shared)
        y_lo = at("y_lo", [ET, T], shared, F32R)
        y_hi = at("y_hi", [ET, T], shared + 32 * KB, F32R)
        v_one = at("v_one", [TB, NB], shared + 64 * KB)
        u_act = at("u_act", [4, T], shared + 68 * KB)
        g_act = at("g_act", [4, T], shared + 72 * KB)
        y_one = at("y_one", [4, T], shared + 76 * KB)
        ws_t = at("ws_t", [TB, G, P], shared + 80 * KB)

        wide_at = top[0]
        wide = new("wide", [LEVELS, T])
        wide4 = wide[:].rearrange("p a t -> p (a t)")
        ws_raw = at("ws_raw", [G, P], wide_at + 4 * KB)
        bs_all = at("bs_all", [G, P], wide_at)
        scan_at = top[0]
        scan = new("scan", [T])
        part = at("part", [T], scan_at)
        ident = new("ident", [P])
        flip = new("flip", [P])
        ones = new("ones", [P])
        p_t = new("p_t", [3 * P])
        vec_rows = at("vec_rows", [2, P], top[0])
        p_n = new("p_n", [3 * P])
        v_head = new("v_head", [TB, DH])
        q_head = new("q_head", [T])
        rstd = at("rstd", [T], top[0])
        hank = new("hank", [T])
        total = new("total", [T])
        vec = new("vec", [2, P])
        lbw = new("lbw", [8, H])
        small = new("small", [64])
        assert top[0] <= nc.sbuf_usable_end, top[0]
        ext_sb = p_t[0:H, 0:EXT]
        GAIN_MIX, GAIN_FFN, GAIN_A, B_GATE, V_GAIN, ROWS0 = 0, 16, 32, 48, 80, 112
        LB0, LB1, OUT_GAIN, Q_GAIN, K_GAIN, ROWS1 = 0, 8, 16, 24, 25, 26
        col = lambda c: vec[:, 0, c:c + 1]
        eps_c, gq_c = small[:, 0:1], small[:, 1:2]
        ssx, rx = small[:, 2:4], small[:, 4:6]
        mneg, psum_, rsum = small[:, 6:8], small[:, 8:10], small[:, 10:12]
        rv, rf = small[:, 12:14], small[:, 14:16]
        ssv = small[:, 16:32].rearrange("p (b g) -> p b g", b=TB)
        ssf = small[:, 32:40].rearrange("p (b g) -> p b g", b=TB)
        tot = small[:, 40:42]
        mpos = small[:, 42:44]

        gp = ctx.enter_context(nc.psum_tensor("gp", [P, 2, 2, NB], F32))
        mx = ctx.enter_context(nc.psum_tensor("mx", [P, 4, NB], F32))

        ext = nc.dram_tensor("ext", [H, EXT], F32, kind="Internal").ap()
        hankel = nc.dram_tensor("hankel", [H, P, T], F32, kind="Internal").ap()

        def sem(name):
            return ctx.enter_context(nc.semaphore(name))

        raw_in = [sem(f"raw_in{s}") for s in range(RING)]
        hi_ready = sem("hi_ready")
        lo_ready = sem("lo_ready")
        unit_used = sem("unit_used")
        bank_free = [sem(f"bank_free{i}") for i in range(2)]
        op_hi = sem("op_hi")
        op_ready = sem("op_ready")
        op_f32 = sem("op_f32")
        x_in = [sem(f"x_in{i}") for i in range(TB)]
        vec_in = sem("vec_in")
        rel_in = sem("rel_in")
        ext_made = sem("ext_made")
        ext_out = sem("ext_out")
        hankel_out = sem("hankel_out")
        consts = sem("consts")
        gp_self = sem("gp_self")
        ones_set = sem("ones_set")
        act_self = sem("act_self")
        dve_self = sem("dve_self")
        xn_ready = sem("xn_ready")
        turned = sem("turned")
        turned_out = sem("turned_out")
        vec_t = sem("vec_t")
        vec_ready = sem("vec_ready")
        lb_exp = sem("lb_exp")
        lb_max = sem("lb_max")
        sums = sem("sums")
        sums2 = sem("sums2")
        rstd_ready = sem("rstd_ready")
        evac_a = sem("evac_a")
        evac_v = sem("evac_v")
        sig_ready = sem("sig_ready")
        pre_ready = sem("pre_ready")
        ln_ready = sem("ln_ready")
        z_ready = sem("z_ready")
        e_ready = sem("e_ready")
        qk_ready = sem("qk_ready")
        prod_done = sem("prod_done")
        p_ready = sem("p_ready")
        cross_copied = sem("cross_copied")
        v_ready = sem("v_ready")
        pv_done = sem("pv_done")
        o_copied = sem("o_copied")
        sq_ready = sem("sq_ready")
        ms_done = sem("ms_done")
        factors_used = sem("factors_used")
        qk_normed = sem("qk_normed")
        norm_part = sem("norm_part")
        hank_in = sem("hank_in")
        s_done = sem("s_done")
        max_done = sem("max_done")
        exp_done = sem("exp_done")
        pn_ready = sem("pn_ready")
        pt_done = sem("pt_done")
        pt_copied = sem("pt_copied")
        ws_in = sem("ws_in")
        bs_in = sem("bs_in")
        ws_turned = sem("ws_turned")
        ws_ready = sem("ws_ready")
        sv_done = sem("sv_done")
        sv_used = sem("sv_used")
        v_one_in = sem("v_one_in")
        y_f32 = sem("y_f32")
        fin_turned = sem("fin_turned")
        fin_copied = sem("fin_copied")
        gain_in = sem("gain_in")
        out_ready = sem("out_ready")
        out_done = sem("out_done")

        a_op, ff_op, y_op = (a_hi, a_lo), (ff_hi, ff_lo), (y_hi, y_lo)
        S = [
            Segment(w_in, "T", 2, D, (0, NB), 2 * NB, a_op),
            Segment(w_in, "N", 2, D, (2 * DM, 2 * DM + NB), 4 * DM, a_op),
            Segment(w_in, "T", 3, D, (3 * DM, 3 * DM + NB), 2 * NB, a_op),
            Segment(w_in, "T", 4, D, (7 * DM, 7 * DM + NB), 2 * NB, a_op),
            Segment(w_proj_a, "T", 2, DM, (0, NB), 2 * NB, a_op),
            Segment(w_proj_b, "T", 2, DM, (0, NB), 2 * NB, a_op, H),
            Segment(w_out, "T", 2, D, (0, NB), 2 * NB, a_op),
            Segment(w_ffn_in, "T", FF // NB, D, (0, FF), NB, a_op),
            Segment(w_ffn_out, "T", 2, FF, (0, NB), 2 * NB, ff_op),
            Segment(a_w_in, "N", 4, D, (E2, E2 + NB), 2 * NB, a_op),
            Segment(a_w_in, "T", G, D, (0, 2 * E2), NB, a_op),
            Segment(a_w_out, "N", 2, E2, (0, NB), 2 * NB, y_op),
        ]
        QF, IV, GQK, GATES, PROJ_A, PROJ_B, OUT, FFN_IN, FFN_OUT, V_IN, UG_IN, Y_OUT = range(len(S))
        unit0, block0 = [0], [0]
        for s in S:
            unit0.append(unit0[-1] + s.steps * s.pair)
            block0.append(block0[-1] + s.steps * 2)
        OPS = {QF: DT, PROJ_A: H + H, OUT: DT, FFN_IN: DT, FFN_OUT: FT, V_IN: DT, Y_OUT: ET}
        op0, n = {}, 0
        for k in range(len(S)):
            op0[k] = n
            n += OPS.get(k, 0)

        def after(k, i, units):
            return i * S[k].pair + (unit0[k] + units)

        block = ctx.enter_context(nc.Block())

        @block.sync
        def _(sp):
            for b in range(TB):
                sp.dma_start(x_tok[:, b], x[b * P:(b + 1) * P, :]).then_inc(x_in[b], 16)

            def load(k, i):
                s = S[k]
                for j in range(s.pair):
                    if (k, i) != (0, 0) or j >= RING:
                        sp.wait_ge(lo_ready, after(k, i, j + 1 - RING))
                    u = j % s.units
                    c = s.first[j // s.units]
                    src = s.w[u * UK * P:(u + 1) * UK * P, bass.ds(i * s.stride + c, NB)]
                    sp.dma_start(raw[:, j % RING], src.rearrange("(k p) n -> p k n", p=P)).then_inc(
                        raw_in[j % RING], 16)

            load(0, 0)
            with sp.Fori(1, S[0].steps) as i:
                load(0, i)
            for k in range(1, len(S)):
                with sp.Fori(0, S[k].steps) as i:
                    load(k, i)
            sp.wait_ge(unit_used, unit0[Y_OUT])
            sp.dma_start(gain_fin[:], final_norm.partition_broadcast(P)).then_inc(gain_in, 16)
            for b in range(TB):
                sp.wait_ge(out_ready, b + 1)
                sp.dma_start(out[b * P:(b + 1) * P, :], x_fin[:, b]).then_inc(out_done, 16)
            sp.wait_ge(out_done, 16 * TB)

        @block.gpsimd
        def _(pool):
            own = Chain(pool, gp_self)
            own.link(pool.memset(ident[:], 0.0))
            own.link(pool.memset(flip[:], 0.0))
            pool.affine_select(out=ident[:], in_=ident[:], compare_op=ALU.not_equal, fill=1.0, base=0,
                               pattern=[[-1, P]], channel_multiplier=1).then_inc(consts, 1)
            pool.affine_select(out=flip[:], in_=flip[:], compare_op=ALU.not_equal, fill=1.0,
                               base=1 - P, pattern=[[1, P]], channel_multiplier=1).then_inc(consts, 1)
            own.link(pool.memset(masks[:], 0.0))
            pool.affine_select(out=masks[:, 0], in_=masks[:, 0], compare_op=ALU.not_equal, fill=1.0,
                               base=0, pattern=[[-1, P]], channel_multiplier=1).then_inc(consts, 1)
            for l in range(MASKED - 1):
                w = 1 << l
                half = masks[:, 1 + l].rearrange("p (b h j) -> p b h j", h=2, j=w)[:, :, 1, :]
                own.link(pool.memset(half, 1.0))
                own.link(pool.affine_select(out=half, in_=half, compare_op=ALU.is_ge, fill=0.0, base=0,
                                            pattern=[[-2 * w, P // (2 * w)], [0, w]], channel_multiplier=1))
                pool.affine_select(out=half, in_=half, compare_op=ALU.is_ge, fill=0.0, base=w - 1,
                                   pattern=[[2 * w, P // (2 * w)], [0, w]],
                                   channel_multiplier=-1).then_inc(consts, 1)

            def hgrn_pool(h):
                pool.wait_ge(e_ready, h + 1)
                for l in range(LEVELS):
                    w = 1 << l
                    two = wide[:, l].rearrange("p (b h j) -> p b h j", h=2, j=w)
                    qh = q_a[:, bass.ds(h, 1)].rearrange("p a (b h j) -> p (a b) h j", h=2, j=w)
                    kh = keys[:, bass.ds(h, 1)].rearrange("p a (b h j) -> p (a b) h j", h=2, j=w)
                    pool.tensor_tensor(two[:, :, 1, :], two[:, :, 1, :], qh[:, :, 1, :], ALU.mult)
                    last = pool.tensor_tensor(two[:, :, 0, :], two[:, :, 0, :], kh[:, :, 0, :], ALU.mult)
                last.then_inc(qk_ready, 1)

            def head_copies(h, which, done):
                pool.wait_ge(pv_done, h + done)
                pool.tensor_copy(v_head[:], val[:, which, :, bass.ds(h * DH, DH)]).then_inc(v_ready, 1)

            pool.wait_ge(ext_made, 1)
            pool.dma_start(ext, ext_sb).then_inc(ext_out, 16)
            pool.wait_ge(ext_out, 16)
            pool.dma_start(hankel, bass.AP(ext.tensor, 0, [[EXT, H], [1, P], [1, T]])).then_inc(hankel_out, 16)
            pool.wait_ge(pre_ready, 2)
            with pool.Fori(0, H) as h:
                head_copies(h, 0, 0)
                pool.tensor_copy(q_head[:], keys[:, bass.ds(h, 1)].rearrange("p a t -> p (a t)")).then_inc(v_ready, 1)
                hgrn_pool(h)
            pool.wait_ge(qk_normed, 1)
            pool.wait_ge(hankel_out, 16)
            with pool.Fori(0, H) as h:
                head_copies(h, 1, H)
                pool.tensor_copy(q_head[:], g_a[:, 1, bass.ds(h, 1)].rearrange("p a t -> p (a t)")).then_inc(v_ready, 1)
                pool.dma_start(hank[:], hankel[bass.ds(h, 1)].rearrange("a p t -> p (a t)")).then_inc(hank_in, 16)
            pool.wait_ge(op_ready, op0[V_IN] + DT)
            pool.dma_start(ws_raw[:], a_w_s.rearrange("g p q -> p g q")).then_inc(ws_in, 16)
            pool.wait_ge(sums, 1)
            pool.dma_start(bs_all[:].rearrange("p g n -> p (g n)"), a_b_s.partition_broadcast(P)).then_inc(bs_in, 16)
            with pool.Fori(0, G) as g:
                pool.wait_ge(sv_done, g)
                pool.tensor_copy(v_one[:], v_g[:, bass.ds(g, 1)].rearrange("p a b n -> p (a b) n")).then_inc(v_one_in, 1)

        @block.scalar
        def _(act):
            own = Chain(act, act_self)

            def split(slot, use, used):
                act.wait_ge(raw_in[slot], use)
                if used is not None:
                    act.wait_ge(unit_used, used)
                act.activation(w_hi[:, slot], raw[:, slot], ACT.Copy).then_inc(hi_ready, 1)

            def step(k, i, evac, last=False):
                s = S[k]
                for j in range(s.pair):
                    if not (last and j >= s.pair - RING):
                        n = unit0[k] + RING + j
                        split(j % RING, i * (16 * s.pair // RING) + 16 * (n // RING + 1),
                              after(k, i, j + 1))
                    if j % s.units == s.units - 1:
                        b = j // s.units
                        act.wait_ge(unit_used, after(k, i, j + 1))
                        evac(i, b)

            def run(k, evac, per=0, final=False):
                steps = S[k].steps - final
                with act.Fori(0, steps) as i:
                    own.enter(i, per)
                    step(k, i, evac)
                    own.leave(steps)
                if final:
                    step(k, steps, evac, last=True)

            def none(i, b):
                pass

            rows = [(0, 0, norm_mix, 16), (0, 16, norm_ffn, 16), (0, 32, a_norm, 16), (0, 48, b_gate, 32),
                    (0, 80, a_v_gain, 32), (1, 0, lb_logits, 16), (1, 16, out_gain, 8), (1, 24, q_gain, 1),
                    (1, 25, k_gain, 1)]
            for which, r, src, n in rows:
                act.dma_start(vec_rows[r:r + n, which], src.rearrange("(r n) -> r n", n=P)).then_inc(vec_in, 16)
            act.dma_start(p_t[0:H, REL_FUTURE + 1:REL_FUTURE + 1 + N_REL], rel_bias).then_inc(rel_in, 16)
            act.wait_ge(ones_set, 1)
            for b in range(TB):
                act.wait_ge(x_in[b], 16)
                own.link(act.activation(wide4, x_tok[:, b], ACT.Square, accum_out=ssx[:, b:b + 1]))
            own.link(act.activation(rx, ssx, ACT.Ln, scale=1.0 / D, bias=eps_c))
            own.link(act.activation(rx, rx, ACT.Exp, scale=-0.5))
            for c in range(2):
                for b in range(TB):
                    if c:
                        act.wait_ge(turned, 4)
                    act.activation(wide4[:, b * D // 2:(b + 1) * D // 2], x_tok[:, b, c * D // 2:(c + 1) * D // 2],
                                   ACT.Copy, scale=rx[:, b:b + 1]).then_inc(xn_ready, 1)
                for g in range(4 * c, 4 * c + 4):
                    for m in (2 * g, 2 * g + 1):
                        if m == 2 * g:
                            act.wait_ge(turned, g + 1)
                            act.wait_ge(vec_ready, 1)
                        act.activation(a_hi[:, m], mx[:, g % 4, (m % 2) * T:(m % 2 + 1) * T], ACT.Copy,
                                       scale=col(GAIN_MIX + m)).then_inc(op_hi, 1)
            for n in range(RING):
                split(n, 16, None)
            for g in range(8):
                act.wait_ge(turned, 9 + g)
                act.activation(x_t[:, 2 * g:2 * g + 2].rearrange("p m t -> p (m t)"), mx[:, g % 4], ACT.Copy).then_inc(
                    turned_out, 1)
            act.wait_ge(lb_max, 1)
            act.activation(lbw[:, 2:4], lbw[:, 2:4], ACT.Exp).then_inc(lb_exp, 1)

            def copy_out(dst):
                def evac(i, b):
                    act.activation(dst(i, b), gp[:, b], ACT.Copy).then_inc(bank_free[b], 1)
                return evac

            run(QF, copy_out(lambda i, b: qf[:, bass.ds(i * 8 + 4 * b, 4)].rearrange("p (a c) t -> p a (c t)", a=2)))
            run(IV, copy_out(lambda i, b: val[:, bass.ds(i, 1), :, b * NB:(b + 1) * NB].rearrange("p a b n -> p (a b) n")))
            run(GQK, copy_out(lambda i, b: g_a[:, bass.ds(i, 1), 4 * b:4 * b + 4].rearrange("p a (b c) t -> p (a b) (c t)", c=2)))

            own.link(act.activation(wide[:], q_a[:], ACT.Sigmoid))
            act.activation(f_a[:], f_a[:], ACT.Sigmoid).then_inc(sig_ready, 1)
            act.wait_ge(pre_ready, 1)
            act.activation(f_a[:], f_a[:], ACT.Ln).then_inc(ln_ready, 1)
            with act.Fori(0, H) as h:
                act.wait_ge(z_ready, h + 1)
                act.activation(wide[:], wide[:], ACT.Exp).then_inc(e_ready, 1)
                act.wait_ge(prod_done, h * 3 + 3)
                act.activation(p_t[:, P:2 * P], mx[:, 3, 0:P], ACT.Copy).then_inc(cross_copied, 1)
                act.wait_ge(pv_done, h + 1)
                act.activation(q_a[:, bass.ds(h, 1)].rearrange("p a t -> p (a t)"), mx[:, 3, T:2 * T], ACT.Copy).then_inc(o_copied, 1)

            def rms(dst, src, dim):
                own.link(act.activation(dst, src, ACT.Ln, scale=1.0 / dim, bias=eps_c))
                act.activation(dst, dst, ACT.Exp, scale=-0.5).then_inc(rstd_ready, 1)

            own_round = [q_a[:], q_b, k_b]
            for r, src in enumerate(own_round):
                if r == 0:
                    act.wait_ge(o_copied, H)
                if r:
                    act.wait_ge(factors_used, r)
                act.activation(wide[:], src, ACT.Square).then_inc(sq_ready, 1)
                act.wait_ge(ms_done, r + 1)
                rms(wide4, mx[:].rearrange("p a n -> p (a n)"), DH)
            act.wait_ge(factors_used, 1)
            act.activation(keys[:], g_a[:, 0], ACT.Sigmoid).then_inc(sig_ready, 1)

            with act.Fori(0, H) as h:
                act.wait_ge(max_done, h + 1)
                act.activation(p_n[:, 0:P], mx[:, 0, 0:P], ACT.Exp, bias=mneg[:, 0:1], accum_out=psum_[:, 0:1])
                act.activation(p_n[:, P:3 * P], mx[:, 0, P:3 * P], ACT.Exp, bias=mneg[:, 1:2],
                               accum_out=psum_[:, 1:2]).then_inc(exp_done, 1)
                act.wait_ge(pt_done, h + 1)
                act.activation(p_t[:], mx[:, 1, 0:3 * P], ACT.Copy).then_inc(pt_copied, 1)
                act.wait_ge(pv_done, h + (H + 1))
                act.activation(g_a[:, 1, bass.ds(h, 1)].rearrange("p a t -> p (a t)"), mx[:, 3, T:2 * T], ACT.Copy).then_inc(o_copied, 1)

            def gate_out(i, b):
                for m in range(4):
                    ins = act.activation(gates[:, bass.ds(i * 8 + (4 * b + m), 1)].rearrange("p a t -> p (a t)"),
                                         gp[:, b, m // 2, (m % 2) * T:(m % 2 + 1) * T], ACT.Sigmoid,
                                         bias=vec[:, 0, bass.ds(i * 8 + (B_GATE + 4 * b + m), 1)])
                ins.then_inc(bank_free[b], 1)

            run(GATES, gate_out)
            act.wait_ge(unit_used, unit0[PROJ_A])
            act.wait_ge(y_f32, 1)
            for src, t in ((q_a, 0), (g_a[:, 1], H)):
                for c in range(2):
                    act.activation(a_hi[:, t + 4 * c:t + 4 * c + 4], src[:, 4 * c:4 * c + 4], ACT.Copy).then_inc(op_hi, 4)
            run(PROJ_A, none)
            run(PROJ_B, none)
            act.wait_ge(unit_used, unit0[OUT])
            for c in range(4):
                act.wait_ge(evac_v, c + 1)
                act.activation(a_hi[:, 4 * c:4 * c + 4], gates[:, 4 * c:4 * c + 4], ACT.Copy).then_inc(op_hi, 4)

            def residual(r):
                def evac(i, b):
                    act.wait_ge(evac_v, i * 2 + (5 + 4 * r + b))
                    act.activation(wide[:, 0:4], x_t[:, bass.ds(i * 8 + 4 * b, 4)], ACT.Square).then_inc(sq_ready, 1)
                return evac

            def next_operand(r, k):
                act.wait_ge(ms_done, 4 + r)
                rms(rstd[:], mx[:, 2, 0:T], D)
                act.wait_ge(unit_used, unit0[k])
                for c in range(4):
                    act.wait_ge(op_f32, 4 * r + c + 1)
                    act.activation(a_hi[:, 4 * c:4 * c + 4], wide[:, 4 * (c % 2):4 * (c % 2) + 4], ACT.Copy).then_inc(op_hi, 4)

            run(OUT, residual(0))
            next_operand(0, FFN_IN)

            def ffn(i, b):
                if b == 0:
                    act.wait_ge(op_ready, i * 4 + op0[FFN_OUT])
                    act.activation(wide[:, 0:4].rearrange("p (a c) t -> p a (c t)", a=2), gp[:, 0], ACT.Silu).then_inc(bank_free[0], 1)
                else:
                    act.wait_ge(y_f32, i + 2)
                    act.activation(ff_hi[:, bass.ds(i * 4, 4)], wide[:, 4:8], ACT.Copy).then_inc(op_hi, 4)

            run(FFN_IN, ffn)
            run(FFN_OUT, residual(1))
            next_operand(1, V_IN)

            act.wait_ge(op_ready, op0[V_IN] + DT)
            def v_out(i, b):
                for t in range(TB):
                    dst = v_g[:, bass.ds(i * 2 + b, 1), t].rearrange("p a n -> p (a n)")
                    own.link(act.activation(dst, gp[:, b, t], ACT.Gelu_apprx_tanh))
                for t in range(TB):
                    dst = v_g[:, bass.ds(i * 2 + b, 1), t].rearrange("p a n -> p (a n)")
                    ins = act.activation(wide4[:, t * NB:(t + 1) * NB], dst, ACT.Square,
                                         accum_out=ssv[:, t, bass.ds(i * 2 + b, 1)])
                own.link(ins)
                act.sem_inc(bank_free[b], 1)

            run(V_IN, v_out, per=6)
            act.sem_inc(sums, 1)
            act.wait_ge(sums2, 1)
            own.link(act.activation(rv, tot, ACT.Ln, scale=1.0 / E2, bias=eps_c))
            own.link(act.activation(rv, rv, ACT.Exp, scale=-0.5))
            act.sem_inc(rstd_ready, 1)

            def ug(i, b):
                if b == 0:
                    act.wait_ge(y_f32, i + (1 + S[FFN_IN].steps))
                    act.activation(u_act[:].rearrange("p (a c) t -> p a (c t)", a=2), gp[:, 0], ACT.Gelu_apprx_tanh).then_inc(bank_free[0], 1)
                else:
                    act.activation(g_act[:].rearrange("p (a c) t -> p a (c t)", a=2), gp[:, 1], ACT.Silu).then_inc(bank_free[1], 1)
                    act.wait_ge(y_f32, i + (2 + S[FFN_IN].steps))
                    act.activation(y_hi[:, bass.ds(i * 4, 4)], y_one[:], ACT.Copy).then_inc(op_hi, 4)

            run(UG_IN, ug)
            for g in range(8):
                act.wait_ge(fin_turned, g + 1)
                b, c = g // 4, g % 4
                act.activation(x_fin[:, b, c * NB:(c + 1) * NB], mx[:, g % 4], ACT.Copy).then_inc(fin_copied, 1)

            def fin(i, b):
                for t in range(TB):
                    if t == 0:
                        act.wait_ge(evac_v, i * 2 + (13 + b))
                    own.link(act.activation(wide4[:, 0:NB], x_fin[:, t, bass.ds(i * 2 * NB + b * NB, NB)], ACT.Square,
                                            accum_out=ssf[:, t, bass.ds(i * 2 + b, 1)]))

            run(Y_OUT, fin, per=4, final=True)
            act.sem_inc(sums, 1)
            act.wait_ge(sums2, 2)
            own.link(act.activation(rf, tot, ACT.Ln, scale=1.0 / D, bias=eps_c))
            own.link(act.activation(rf, rf, ACT.Exp, scale=-0.5))
            act.sem_inc(rstd_ready, 1)

        @block.vector
        def _(dve):
            own = Chain(dve, dve_self)

            def split(slot, n):
                dve.wait_ge(hi_ready, n)
                dve.tensor_tensor(w_lo[:, slot], raw[:, slot], w_hi[:, slot], ALU.subtract).then_inc(lo_ready, 1)

            def step(k, i, evac, last=False):
                s = S[k]
                for j in range(s.pair):
                    if not (last and j >= s.pair - RING):
                        split(j % RING, after(k, i, RING + j + 1))
                    if j % s.units == s.units - 1:
                        b = j // s.units
                        dve.wait_ge(unit_used, after(k, i, j + 1))
                        evac(i, b)

            def run(k, evac, per=0, final=False):
                steps = S[k].steps - final
                with dve.Fori(0, steps) as i:
                    own.enter(i, per)
                    step(k, i, evac)
                    own.leave(steps)
                if final:
                    step(k, steps, evac, last=True)

            def none(i, b):
                pass

            dve.memset(small[:, 0:1], EPS)
            dve.memset(gp[:, 0, 0, 0:1], 0.0).then_inc(bank_free[0], 1)
            dve.memset(gp[:, 1, 0, 0:1], 0.0).then_inc(bank_free[1], 1)
            dve.memset(ones[:], 1.0).then_inc(ones_set, 1)
            dve.wait_ge(rel_in, 16)
            dve.tensor_copy(ext_sb[:, 0:REL_FUTURE + 1], ext_sb[:, REL_FUTURE + 1:REL_FUTURE + 2].broadcast_to([H, REL_FUTURE + 1]))
            e = REL_FUTURE + 1 + N_REL
            dve.tensor_copy(ext_sb[:, e:EXT], ext_sb[:, e - 1:e].broadcast_to([H, EXT - e])).then_inc(ext_made, 1)
            dve.wait_ge(vec_t, 1)
            own.link(dve.tensor_copy(vec[:, 0, 0:ROWS0], mx[:, 0, 0:ROWS0]))
            own.link(dve.tensor_copy(vec[:, 1, 0:ROWS1], mx[:, 1, 0:ROWS1]))
            dve.tensor_scalar(gq_c, vec[:, 1, Q_GAIN:Q_GAIN + 1], DH ** -0.5, None, ALU.mult).then_inc(vec_ready, 1)
            for g in range(8):
                for m in (2 * g, 2 * g + 1):
                    dve.wait_ge(op_hi, 2 * g + 2)
                    dve.scalar_tensor_tensor(out=a_lo[:, m], in0=mx[:, g % 4, (m % 2) * T:(m % 2 + 1) * T],
                                             scalar=col(GAIN_MIX + m), in1=a_hi[:, m].bitcast(F32), op0=ALU.mult,
                                             op1=ALU.subtract).then_inc(op_ready, 1)
            for n in range(RING):
                split(n, n + 1)
            l0, l1 = vec[:, 1, LB0:LB0 + H], vec[:, 1, LB1:LB1 + H]
            own.link(dve.tensor_tensor(lbw[:, 0], l0, l1, ALU.max))
            dve.tensor_tensor(lbw[:, 2], l0, lbw[:, 0], ALU.subtract)
            dve.tensor_tensor(lbw[:, 3], l1, lbw[:, 0], ALU.subtract).then_inc(lb_max, 1)
            dve.wait_ge(lb_exp, 1)
            own.link(dve.tensor_tensor(lbw[:, 0], lbw[:, 2], lbw[:, 3], ALU.add))
            own.link(dve.reciprocal(lbw[:, 1], lbw[:, 0]))
            own.link(dve.tensor_tensor(lbw[:, 4], lbw[:, 2], lbw[:, 1], ALU.mult))
            own.link(dve.tensor_scalar(lbw[:, 5], lbw[:, 4], -1.0, 1.0, ALU.mult, ALU.add))

            run(QF, none)
            run(IV, none)
            run(GQK, none)

            dve.wait_ge(sig_ready, 1)
            for h in range(H):
                ins = dve.tensor_scalar(f_a[:, h], f_a[:, h], lbw[:, 5, h:h + 1], lbw[:, 4, h:h + 1], ALU.mult, ALU.add)
            own.link(ins)
            own.link(dve.tensor_scalar(keys[:], f_a[:], -1.0, 1.0, ALU.mult, ALU.add))
            dve.tensor_scalar(f_a[:], f_a[:], LN_MIN, None, ALU.max).then_inc(pre_ready, 1)
            dve.tensor_tensor(q_a[:], q_a[:], wide[:], ALU.mult).then_inc(pre_ready, 1)
            dve.wait_ge(consts, 2 + MASKED)
            dve.wait_ge(ln_ready, 1)
            dve.wait_ge(pre_ready, 2)

            def decays(h):
                lf = f_a[:, bass.ds(h, 1)].rearrange("p a t -> p (a t)")
                for c in range(T // CHUNK):
                    c0, c1 = c * CHUNK, (c + 1) * CHUNK
                    ins = dve.tensor_tensor_scan(scan[:, c0:c1], ones[:, 0:CHUNK], lf[:, c0:c1], 0.0, ALU.mult, ALU.add)
                own.link(ins)
                for l in range(LEVELS - 1):
                    w = 1 << l
                    b4 = scan[:].rearrange("p (b h j) -> p b h j", h=2, j=w)
                    z4 = wide[:, l].rearrange("p (b h j) -> p b h j", h=2, j=w)
                    ref = b4[:, :, 0, w - 1:w].broadcast_to([P, T // (2 * w), w])
                    if w < CHUNK:
                        dve.tensor_tensor(z4[:, :, 1, :], b4[:, :, 1, :], ref, ALU.subtract)
                    else:
                        dve.tensor_copy(z4[:, :, 1, :], b4[:, :, 1, :])
                    dve.tensor_tensor(z4[:, :, 0, :], ref, b4[:, :, 0, :], ALU.subtract)
                z, c1, c2, c3 = wide[:, LEVELS - 1], CHUNK, 2 * CHUNK, 3 * CHUNK
                dve.tensor_scalar(z[:, c1:c2], scan[:, c1:c2], scan[:, c2 - 1:c2], -1.0, ALU.subtract, ALU.mult)
                dve.tensor_copy(z[:, c2:c3], scan[:, c2:c3])
                dve.tensor_scalar(z[:, c3:T], scan[:, c3:T], scan[:, c3 - 1:c3], None, ALU.add)
                own.link(dve.tensor_scalar(z[:, 0:c1], scan[:, 0:c1], scan[:, c1 - 1:c1], -1.0, ALU.subtract, ALU.mult))
                dve.tensor_scalar(z[:, 0:c1], z[:, 0:c1], scan[:, c2 - 1:c2], None, ALU.add).then_inc(z_ready, 1)

            def scores(h, b):
                dve.wait_ge(prod_done, h * 3 + (b + 1))
                part8 = mx[:, 0:2].rearrange("p a n -> p (a n)")
                own.link(dve.tensor_tensor(masked[:].rearrange("p l t -> p (l t)"), part8[:, 0:MASKED * P],
                                           masks[:].rearrange("p l t -> p (l t)"), ALU.mult))
                dst = p_t[:, 2 * b * P:(2 * b + 1) * P]
                own.link(dve.tensor_reduce(dst, masked[:].rearrange("p l t -> p t l"), AX_X, ALU.add))
                dve.tensor_tensor(dst[0:CHUNK, CHUNK:P], dst[0:CHUNK, CHUNK:P],
                                  part8[0:CHUNK, MASKED * P:MASKED * P + CHUNK], ALU.add).then_inc(p_ready, 1)

            with dve.Fori(0, H) as h:
                own.enter(h, 6)
                dve.wait_ge(o_copied, h)
                decays(h)
                scores(h, 0)
                scores(h, 1)
                own.leave(H)

            dve.wait_ge(rstd_ready, 1)
            for h in range(H):
                ins = dve.scalar_tensor_tensor(out=q_a[:, h], in0=q_a[:, h], scalar=vec[:, 1, OUT_GAIN + h:OUT_GAIN + h + 1],
                                               in1=wide[:, h], op0=ALU.mult, op1=ALU.mult)
            ins.then_inc(factors_used, 1)
            dve.wait_ge(rstd_ready, 2)
            dve.scalar_tensor_tensor(out=q_b.rearrange("p h t -> p (h t)"), in0=q_b.rearrange("p h t -> p (h t)"),
                                     scalar=gq_c, in1=wide4, op0=ALU.mult, op1=ALU.mult).then_inc(factors_used, 1)
            dve.wait_ge(rstd_ready, 3)
            dve.wait_ge(factors_used, 2)
            dve.scalar_tensor_tensor(out=k_b.rearrange("p h t -> p (h t)"), in0=k_b.rearrange("p h t -> p (h t)"),
                                     scalar=vec[:, 1, K_GAIN:K_GAIN + 1], in1=wide4, op0=ALU.mult,
                                     op1=ALU.mult).then_inc(qk_normed, 1)
            dve.wait_ge(sig_ready, 2)
            own.link(dve.tensor_tensor(keys[:], keys[:], g_a[:, 0], ALU.mult))
            dve.tensor_tensor(q_a[:], q_a[:], keys[:], ALU.mult).then_inc(y_f32, 1)

            with dve.Fori(0, H) as h:
                own.enter(h, 4)
                dve.wait_ge(s_done, h + 1)
                s3 = mx[:, 0, 0:3 * P]
                hidden = mx[0:CHUNK, 0, 0:3 * P].rearrange("p (a n) -> p a n", n=P)[:, 0:3:2, CHUNK:P]
                own.link(dve.memset(hidden, NEG))
                dve.tensor_reduce(mpos[:, 0:1], s3[:, 0:P], AX_X, ALU.max)
                own.link(dve.tensor_reduce(mpos[:, 1:2], s3[:, P:3 * P], AX_X, ALU.max))
                dve.tensor_scalar(mneg, mpos, -1.0, None, ALU.mult).then_inc(max_done, 1)
                dve.wait_ge(exp_done, h + 1)
                own.link(dve.reciprocal(rsum, psum_))
                dve.tensor_scalar(p_n[:, 0:P], p_n[:, 0:P], rsum[:, 0:1], None, ALU.mult)
                own.link(dve.tensor_scalar(p_n[:, P:3 * P], p_n[:, P:3 * P], rsum[:, 1:2], None, ALU.mult))
                dve.sem_inc(pn_ready, 1)
                own.leave(H)

            run(GATES, none)
            dve.wait_ge(o_copied, 2 * H)
            for src, t in ((q_a, 0), (g_a[:, 1], H)):
                for c in range(2):
                    t0 = t + 4 * c
                    dve.wait_ge(op_hi, op0[PROJ_A] + t0 + 4)
                    dve.tensor_tensor(a_lo[:, t0:t0 + 4], src[:, 4 * c:4 * c + 4], a_hi[:, t0:t0 + 4].bitcast(F32),
                                      ALU.subtract).then_inc(op_ready, 4)

            def proj_a(i, b):
                g4 = gates[:, bass.ds(i * 8 + 4 * b, 4)].rearrange("p (a c) t -> p a (c t)", a=2)
                dve.tensor_tensor(g4, gp[:, b], g4, ALU.mult).then_inc(bank_free[b], 1)

            def proj_b(i, b):
                ga = gates[:, bass.ds(i * 8 + 4 * b, 4)].rearrange("p (a c) t -> p a (c t)", a=2)
                gb = gates[:, bass.ds(i * 8 + (DT + 4 * b), 4)].rearrange("p (a c) t -> p a (c t)", a=2)
                own.link(dve.tensor_tensor(gb, gp[:, b], gb, ALU.mult))
                dve.sem_inc(bank_free[b], 1)
                dve.tensor_tensor(ga, ga, gb, ALU.add).then_inc(evac_v, 1)

            run(PROJ_A, proj_a)
            run(PROJ_B, proj_b, per=2)
            for c in range(4):
                dve.wait_ge(op_hi, op0[OUT] + 4 * c + 4)
                dve.tensor_tensor(a_lo[:, 4 * c:4 * c + 4], gates[:, 4 * c:4 * c + 4],
                                  a_hi[:, 4 * c:4 * c + 4].bitcast(F32), ALU.subtract).then_inc(op_ready, 4)

            def residual(r):
                def evac(i, b):
                    x4 = x_t[:, bass.ds(i * 8 + 4 * b, 4)].rearrange("p (a c) t -> p a (c t)", a=2)
                    own.link(dve.tensor_tensor(x4, gp[:, b], x4, ALU.add))
                    dve.sem_inc(evac_v, 1)
                    dve.sem_inc(bank_free[b], 1)
                    dve.wait_ge(sq_ready, i * 2 + (4 + 4 * r + b))
                    own.link(dve.tensor_reduce(part[:], wide[:, 0:4].rearrange("p m t -> p t m"), AX_X, ALU.add))
                    own.link(dve.tensor_tensor(total[:], total[:], part[:], ALU.add))
                return evac

            def next_operand(r, gain, k):
                dve.wait_ge(rstd_ready, 4 + r)
                for c in range(4):
                    if c >= 2:
                        dve.wait_ge(op_ready, op0[k] + 4 * (c - 1))
                    for m in range(4 * c, 4 * c + 4):
                        ins = dve.scalar_tensor_tensor(out=wide[:, m % 8], in0=x_t[:, m], scalar=col(gain + m),
                                                       in1=rstd[:], op0=ALU.mult, op1=ALU.mult)
                    ins.then_inc(op_f32, 1)
                    dve.wait_ge(op_hi, op0[k] + 4 * c + 4)
                    dve.tensor_tensor(a_lo[:, 4 * c:4 * c + 4], wide[:, 4 * (c % 2):4 * (c % 2) + 4],
                                      a_hi[:, 4 * c:4 * c + 4].bitcast(F32), ALU.subtract).then_inc(op_ready, 4)

            own.link(dve.memset(total[:], 0.0))
            run(OUT, residual(0), per=6)
            dve.sem_inc(norm_part, 1)
            next_operand(0, GAIN_FFN, FFN_IN)

            def ffn(i, b):
                if b == 0:
                    return
                dve.wait_ge(bank_free[0], i + (block0[FFN_IN] // 2 + 2))
                up = wide[:, 4:8].rearrange("p (a c) t -> p a (c t)", a=2)
                own.link(dve.tensor_tensor(up, gp[:, 1], wide[:, 0:4].rearrange("p (a c) t -> p a (c t)", a=2), ALU.mult))
                dve.sem_inc(bank_free[1], 1)
                dve.sem_inc(y_f32, 1)
                dve.wait_ge(op_hi, i * 4 + (op0[FFN_OUT] + 4))
                dve.tensor_tensor(ff_lo[:, bass.ds(i * 4, 4)], wide[:, 4:8], ff_hi[:, bass.ds(i * 4, 4)].bitcast(F32),
                                  ALU.subtract).then_inc(op_ready, 4)

            run(FFN_IN, ffn, per=1)
            own.link(dve.memset(total[:], 0.0))
            run(FFN_OUT, residual(1), per=6)
            dve.sem_inc(norm_part, 1)
            next_operand(1, GAIN_A, V_IN)

            run(V_IN, none)
            dve.wait_ge(sums, 1)
            own.link(dve.tensor_reduce(tot, ssv, AX_X, ALU.add))
            dve.sem_inc(sums2, 1)
            dve.wait_ge(rstd_ready, 6)
            dve.wait_ge(ws_turned, 1)
            dve.wait_ge(bs_in, 16)
            for t in range(TB):
                ins = dve.tensor_scalar(ws_t[:, t].rearrange("p g n -> p (g n)"),
                                        mx[:, 0:2].rearrange("p a n -> p (a n)"), rv[:, t:t + 1], None, ALU.mult)
            ins.then_inc(ws_ready, 1)

            def ug(i, b):
                if b == 0:
                    dve.wait_ge(sv_done, i + 1)
                    dve.wait_ge(op_hi, i * 4 + op0[Y_OUT])
                    for c in range(4):
                        ins = dve.scalar_tensor_tensor(
                            out=y_one[:, c].rearrange("p (b t) -> p b t", b=TB),
                            in0=mx[:, c // 2, (c % 2) * T:(c % 2 + 1) * T].rearrange("p (b t) -> p b t", b=TB),
                            scalar=vec[:, 0, bass.ds(i * 4 + (V_GAIN + c), 1)],
                            in1=bs_all[:, bass.ds(i, 1)].broadcast_to([P, TB, P]), op0=ALU.mult, op1=ALU.add)
                    own.link(ins)
                    dve.sem_inc(sv_used, 1)
                    dve.wait_ge(bank_free[0], i + (block0[UG_IN] // 2 + 2))
                    own.link(dve.tensor_tensor(y_one[:], y_one[:], u_act[:], ALU.mult))
                else:
                    dve.wait_ge(bank_free[1], i + (block0[UG_IN] // 2 + 2))
                    own.link(dve.tensor_tensor(y_one[:], y_one[:], g_act[:], ALU.mult))
                    dve.sem_inc(y_f32, 1)
                    dve.wait_ge(op_hi, i * 4 + (op0[Y_OUT] + 4))
                    dve.tensor_tensor(y_lo[:, bass.ds(i * 4, 4)], y_one[:], y_hi[:, bass.ds(i * 4, 4)].bitcast(F32),
                                      ALU.subtract).then_inc(op_ready, 4)

            run(UG_IN, ug, per=3)

            def fin(i, b):
                if not isinstance(i, int) and b == 0:
                    dve.wait_ge(fin_copied, 8)
                xf = x_fin[:, :, bass.ds(i * 2 * NB + b * NB, NB)]
                own.link(dve.tensor_tensor(xf, gp[:, b], xf, ALU.add))
                dve.sem_inc(evac_v, 1)
                dve.sem_inc(bank_free[b], 1)

            run(Y_OUT, fin, per=2, final=True)
            dve.wait_ge(sums, 2)
            own.link(dve.tensor_reduce(tot, ssf, AX_X, ALU.add))
            dve.sem_inc(sums2, 1)
            dve.wait_ge(rstd_ready, 7)
            dve.wait_ge(gain_in, 16)
            for b in range(TB):
                dve.scalar_tensor_tensor(out=x_fin[:, b], in0=x_fin[:, b], scalar=rf[:, b:b + 1], in1=gain_fin[:],
                                         op0=ALU.mult, op1=ALU.mult).then_inc(out_ready, 1)

        @block.tensor
        def _(pe):
            def unit(k, i, j):
                s = S[k]
                hi, lo = s.operand
                b, u, slot = j // s.units, j % s.units, j % RING
                pe.wait_ge(lo_ready, after(k, i, j + 1))
                for kk in range(UK):
                    t = s.tile0 + u * UK + kk
                    first = u == 0 and kk == 0
                    last = u == s.units - 1 and kk == UK - 1
                    for m in range(4 if s.form == "T" else 2):
                        for p, (wp, ap) in enumerate(((w_hi, hi), (w_hi, lo), (w_lo, hi))):
                            if s.form == "T":
                                out_ = gp[:, b, m // 2, (m % 2) * T:(m % 2 + 1) * T]
                                stat, mov = wp[:, slot, kk, m * P:(m + 1) * P], ap[:, t, :]
                                start = first and m % 2 == 0 and p == 0
                            else:
                                out_ = gp[:, b, m, :]
                                stat, mov = ap[:, t, m * P:(m + 1) * P], wp[:, slot, kk, :]
                                start = first and p == 0
                            ins = pe.matmul(out_, stat, mov, start=start, stop=last and p == 2, skip_group_check=True)
                ins.then_inc(unit_used, 1)

            def run(k, operand=None, mid=None):
                s = S[k]
                with pe.Fori(0, s.steps) as i:
                    for j in range(s.pair):
                        if j % s.units == 0:
                            b = j // s.units
                            pe.wait_ge(bank_free[b], i + (block0[k] // 2 + 1))
                        if operand is not None:
                            pe.wait_ge(op_ready, operand + min(s.tile0 % DT + (j % s.units + 1) * UK, OPS_MAX[k]))
                        unit(k, i, j)
                        if mid is not None:
                            mid(i, j)

            OPS_MAX = {QF: DT, PROJ_A: H, PROJ_B: 2 * H, OUT: DT, FFN_IN: DT, V_IN: DT}

            pe.wait_ge(consts, 2)
            pe.wait_ge(vec_in, 16 * 9)
            pe.transpose(mx[:, 0, 0:ROWS0], vec_rows[0:ROWS0, 0], ident[0:ROWS0, 0:ROWS0])
            pe.transpose(mx[:, 1, 0:ROWS1], vec_rows[0:ROWS1, 1], ident[0:ROWS1, 0:ROWS1]).then_inc(vec_t, 1)
            pe.wait_ge(vec_ready, 1)
            for g in range(8):
                if g >= 4:
                    pe.wait_ge(op_ready, 2 * (g - 3))
                pe.wait_ge(xn_ready, 2 * (g // 4) + 2)
                for m in (2 * g, 2 * g + 1):
                    for b in range(TB):
                        c0 = b * D // 2 + (m % 8) * P
                        ins = pe.transpose(mx[:, g % 4, (m % 2) * T + b * P:(m % 2) * T + (b + 1) * P],
                                           wide4[:, c0:c0 + P], ident[:])
                ins.then_inc(turned, 1)
            for g in range(8):
                pe.wait_ge(op_ready, min(2 * (g + 5), 16))
                if g >= 4:
                    pe.wait_ge(turned_out, g - 3)
                for m in (2 * g, 2 * g + 1):
                    for b in range(TB):
                        ins = pe.transpose(mx[:, g % 4, (m % 2) * T + b * P:(m % 2) * T + (b + 1) * P],
                                           x_tok[:, b, m * P:(m + 1) * P], ident[:])
                ins.then_inc(turned, 1)

            run(QF, op0[QF])
            run(IV)
            run(GQK)

            def level_products(h, b):
                tb = slice(b * P, (b + 1) * P)
                if b == 0:
                    pe.wait_ge(qk_ready, h + 1)
                    pe.wait_ge(v_ready, h * 2 + 2)
                pe.wait_ge(p_ready, h * 2 + b)
                part8 = mx[:, 0:2].rearrange("p a n -> p (a n)")
                pe.matmul(part8[:, 0:P], q_head[:, tb], q_a[:, bass.ds(h, 1), tb].rearrange("p a t -> p (a t)"),
                          start=True, stop=True, skip_group_check=True)
                for l in range(MASKED - 1):
                    pe.matmul(part8[:, (l + 1) * P:(l + 2) * P], wide[:, l, tb], wide[:, l, tb],
                              start=l == 3, stop=True, skip_group_check=True)
                c0 = b * P
                pe.matmul(part8[0:CHUNK, MASKED * P:MASKED * P + CHUNK], wide[:, LEVELS - 2, c0:c0 + CHUNK],
                          wide[:, LEVELS - 2, c0 + CHUNK:c0 + P], start=False, stop=True,
                          skip_group_check=True).then_inc(prod_done, 1)

            def values(ready):
                pe.matmul(mx[:, 3, T:2 * T], v_head[:, 0], p_t[:, 0:T], start=True, stop=False, skip_group_check=True)
                pe.matmul(mx[:, 3, T + P:2 * T], v_head[:, 1], p_t[:, T:3 * P], start=False, stop=True,
                          skip_group_check=True).then_inc(pv_done, 1)

            with pe.Fori(0, H) as h:
                level_products(h, 0)
                level_products(h, 1)
                pe.wait_ge(o_copied, h)
                pe.matmul(mx[:, 3, 0:P], wide[:, LEVELS - 1, 0:P], wide[:, LEVELS - 1, P:T], start=True, stop=True,
                          skip_group_check=True).then_inc(prod_done, 1)
                pe.wait_ge(p_ready, h * 2 + 2)
                pe.wait_ge(cross_copied, h + 1)
                values(h)

            for r in range(3):
                pe.wait_ge(sq_ready, r + 1)
                pe.wait_ge(o_copied, H)
                for b in range(4):
                    ins = pe.matmul(mx[:, b], ones[:], wide4[:, b * NB:(b + 1) * NB], start=True, stop=True,
                                    skip_group_check=True)
                ins.then_inc(ms_done, 1)

            pe.wait_ge(qk_normed, 1)
            with pe.Fori(0, H) as h:
                pe.wait_ge(hank_in, h * 16 + 16)
                pe.wait_ge(v_ready, h * 2 + (2 * H + 2))
                pe.wait_ge(exp_done, h)
                kh = g_a[:, 2, bass.ds(h, 1)].rearrange("p a t -> p (a t)")
                s_ = mx[:, 0]
                pe.matmul(s_[:, 0:P], hank[:, 0:P], flip[:], start=True, stop=False, skip_group_check=True)
                pe.matmul(s_[:, P:2 * P], hank[:, P:T], flip[:], start=False, stop=False, skip_group_check=True)
                pe.matmul(s_[:, 2 * P:3 * P], hank[:, 0:P], flip[:], start=False, stop=False, skip_group_check=True)
                pe.matmul(s_[:, 0:P], q_head[:, 0:P], kh[:, 0:P], start=False, stop=True, skip_group_check=True)
                pe.matmul(s_[:, P:3 * P], q_head[:, P:T], kh, start=False, stop=True,
                          skip_group_check=True).then_inc(s_done, 1)
                pe.wait_ge(pn_ready, h + 1)
                for c in range(3):
                    ins = pe.transpose(mx[:, 1, c * P:(c + 1) * P], p_n[:, c * P:(c + 1) * P], ident[:])
                ins.then_inc(pt_done, 1)
                pe.wait_ge(pt_copied, h + 1)
                pe.wait_ge(o_copied, h + H)
                values(h)

            run(GATES)
            run(PROJ_A, op0[PROJ_A])
            run(PROJ_B, op0[PROJ_A])

            def norm_sum(r):
                pe.wait_ge(norm_part, r + 1)
                pe.matmul(mx[:, 2, 0:T], ones[:], total[:], start=True, stop=True).then_inc(ms_done, 1)

            run(OUT, op0[OUT])
            norm_sum(0)
            run(FFN_IN, op0[FFN_IN])
            pe.wait_ge(op_ready, op0[FFN_OUT] + FT)
            run(FFN_OUT)
            norm_sum(1)
            run(V_IN, op0[V_IN])
            pe.wait_ge(ws_in, 16)
            for g in range(G):
                ins = pe.transpose(mx[:, g // 4, (g % 4) * P:(g % 4 + 1) * P], ws_raw[:, g], ident[:])
            ins.then_inc(ws_turned, 1)
            pe.wait_ge(ws_ready, 1)

            def mix(g, j):
                if j != 2:
                    return
                pe.wait_ge(v_one_in, g + 1)
                pe.wait_ge(sv_used, g)
                for c in range(4):
                    for b in range(TB):
                        t0 = (c % 2) * T + b * P
                        ins = pe.matmul(mx[:, c // 2, t0:t0 + P], v_one[:, b, c * P:(c + 1) * P],
                                        ws_t[:, b, bass.ds(g, 1)].rearrange("p a n -> p (a n)"),
                                        start=True, stop=True, skip_group_check=True)
                ins.then_inc(sv_done, 1)

            run(UG_IN, mid=mix)
            for g in range(8):
                if g >= 4:
                    pe.wait_ge(fin_copied, g - 3)
                if g == 0:
                    pe.wait_ge(sv_used, G)
                b, c = g // 4, g % 4
                for m in range(4):
                    ins = pe.transpose(mx[:, g % 4, m * P:(m + 1) * P], x_t[:, 4 * c + m, b * P:(b + 1) * P], ident[:])
                ins.then_inc(fin_turned, 1)
            pe.wait_ge(op_ready, op0[Y_OUT] + ET)
            run(Y_OUT)


def kernel(**inputs):
    import numpy as np
    import concourse.bacc as bacc
    from concourse.bass_utils import run_bass_kernel_spmd

    nc = bacc.Bacc("TRN2", target_bir_lowering=False, num_devices=1)
    arrays = {}

    def given(name):
        a = np.ascontiguousarray(inputs[name])
        arrays[name + "_in"] = a
        return nc.dram_tensor(name + "_in", a.shape, F32, kind="ExternalInput").ap()

    one = lambda name: given(name)[0]
    out = nc.dram_tensor("result", [1, T, D], F32, kind="ExternalOutput").ap()
    build(nc, one("x"), one("w_in"), one("b_gate"), one("norm_mix"), one("norm_ffn"),
          given("hgrn_lb_logits").rearrange("a n -> (a n)"), one("hgrn_out_gain"), one("q_gain"), one("k_gain"),
          one("rel_bias"), one("w_proj_a"), one("w_proj_b"), one("w_out"), one("w_ffn_in"), one("w_ffn_out"),
          one("a_norm_2"), one("a_w_in_2"), one("a_v_gain_2"), one("a_w_s_2"),
          one("a_b_s_2").rearrange("g n -> (g n)"), one("a_w_out_2"), given("final_norm_2"), out[0])
    got = run_bass_kernel_spmd(nc, [arrays], core_ids=[0])
    return got.results[0]["result"]
```

```python
from contextlib import ExitStack

import concourse.bass as bass
from concourse import mybir

ALU = mybir.AluOpType
ACT = mybir.ActivationFunctionType
F32 = mybir.dt.float32
F32R = mybir.dt.float32r
AX_X = mybir.AxisListType.X

P = 128
T = 256
TB = T // P
D = 2048
DT = D // P
H = 8
DH = 128
DM = H * DH
CHUNK = 64
N_REL = 191
REL_FUTURE = CHUNK - 1
FF = 5632
FT = FF // P
E2 = 4096
ET = E2 // P
G = 8
EPS = 1e-6
NEG = -3.0e38
LN_MIN = 2.0 ** -64

NB = 512
UK = 2
RING = 4
LEVELS = 8
MASKED = 7
EXT = 384


class Segment:

    def __init__(self, weights, form, steps, rows, first, stride, operand, tile0=0):
        self.w, self.form, self.steps, self.units = weights, form, steps, rows // (UK * P)
        self.first, self.stride = first, stride
        self.operand, self.tile0 = operand, tile0
        self.pair = 2 * self.units
        assert self.pair % RING == 0


class Chain:

    def __init__(self, eng, sem):
        self.eng, self.sem, self.base, self.step, self.at = eng, sem, 0, 0, 0

    def value(self):
        return self.at + self.base if not self.step else self.step[0] * self.step[1] + (self.base + self.at)

    def link(self, instruction):
        instruction.then_inc(self.sem, 1)
        self.at += 1
        self.eng.wait_ge(self.sem, self.value())

    def enter(self, i, per):
        self.base, self.at, self.step = self.base + self.at, 0, (i, per)

    def leave(self, steps):
        assert self.at == self.step[1], (self.at, self.step[1])
        self.base, self.at, self.step = self.base + steps * self.step[1], 0, 0


def build(nc, x, w_in, b_gate, norm_mix, norm_ffn, lb_logits, out_gain, q_gain, k_gain, rel_bias,
          w_proj_a, w_proj_b, w_out, w_ffn_in, w_ffn_out, a_norm, a_w_in, a_v_gain, a_w_s, a_b_s,
          a_w_out, final_norm, out):
    ctx = ExitStack()
    with ctx:
        top = [(nc.sbuf_base + 63) // 64 * 64]

        def at(name, shape, offset, dt=F32):
            return nc.alloc_sbuf_tensor_at(name, [P] + shape, dt, offset=offset)

        def size(shape):
            n = 4
            for s in shape:
                n *= s
            return n

        def new(name, shape, dt=F32):
            offset = top[0]
            top[0] += (size(shape) + 31) // 32 * 32
            return at(name, shape, offset, dt)

        raw = new("raw", [RING, UK, NB])
        w_hi = new("w_hi", [RING, UK, NB], F32R)
        w_lo = new("w_lo", [RING, UK, NB], F32R)
        a_at = top[0]
        a_hi = new("a_hi", [DT, T], F32R)
        a_lo = new("a_lo", [DT, T], F32R)
        x_t = new("x_t", [DT, T])
        x_fin = at("x_fin", [TB, D], a_at)
        gain_fin = at("gain_fin", [D], a_at + size([TB, D]))

        shared = top[0]
        top[0] += 88 * 1024
        KB = 1024
        qf = at("qf", [2 * H, T], shared)
        q_a = qf[:, 0:H]
        f_a = qf[:, H:2 * H]
        g_a = at("g_a", [3, H, T], shared + 16 * KB)
        q_b, k_b = g_a[:, 1], g_a[:, 2]
        val = at("val", [2, TB, DM], shared + 40 * KB)
        gates = at("gates", [2 * DT, T], shared + 56 * KB)
        wide_b = at("wide_b", [LEVELS, T], shared + 64 * KB)
        x_tok = at("x_tok", [TB, D], shared + 56 * KB)
        keys = at("keys", [H, T], shared + 72 * KB)
        masks = at("masks", [MASKED, P], shared + 80 * KB)
        masked = at("masked", [MASKED, P], shared + 80 * KB + size([MASKED, P]))
        ff_hi = at("ff_hi", [FT, T], shared, F32R)
        ff_lo = at("ff_lo", [FT, T], shared + 44 * KB, F32R)
        v_g = at("v_g", [G, TB, NB], shared)
        y_lo = at("y_lo", [ET, T], shared, F32R)
        y_hi = at("y_hi", [ET, T], shared + 32 * KB, F32R)
        v_one = at("v_one", [TB, NB], shared + 64 * KB)
        u_act = at("u_act", [4, T], shared + 68 * KB)
        g_act = at("g_act", [4, T], shared + 72 * KB)
        y_one = at("y_one", [4, T], shared + 76 * KB)
        ws_t = at("ws_t", [TB, G, P], shared + 80 * KB)

        wide_at = top[0]
        wide = new("wide", [LEVELS, T])
        wide4 = wide[:].rearrange("p a t -> p (a t)")
        ws_raw = at("ws_raw", [G, P], wide_at + 4 * KB)
        bs_all = at("bs_all", [G, P], wide_at)
        scan_at = top[0]
        scan = new("scan", [T])
        part = at("part", [T], scan_at)
        ident = new("ident", [P])
        flip = new("flip", [P])
        ones = new("ones", [P])
        p_t = new("p_t", [3 * P])
        vec_rows = at("vec_rows", [2, P], top[0])
        p_n = new("p_n", [3 * P])
        v_head = new("v_head", [TB, DH])
        q_head = new("q_head", [T])
        rstd = at("rstd", [T], top[0])
        hank = new("hank", [T])
        total = new("total", [T])
        vec = new("vec", [2, P])
        lbw = new("lbw", [8, H])
        small = new("small", [64])
        assert top[0] <= nc.sbuf_usable_end, top[0]
        ext_sb = p_t[0:H, 0:EXT]
        decay = [wide, wide_b]
        key_head = [q_head, hank]
        GAIN_MIX, GAIN_FFN, GAIN_A, B_GATE, V_GAIN, ROWS0 = 0, 16, 32, 48, 80, 112
        LB0, LB1, OUT_GAIN, Q_GAIN, K_GAIN, ROWS1 = 0, 8, 16, 24, 25, 26
        col = lambda c: vec[:, 0, c:c + 1]
        eps_c, gq_c = small[:, 0:1], small[:, 1:2]
        ssx, rx = small[:, 2:4], small[:, 4:6]
        mneg, psum_, rsum = small[:, 6:8], small[:, 8:10], small[:, 10:12]
        rv, rf = small[:, 12:14], small[:, 14:16]
        ssv = small[:, 16:32].rearrange("p (b g) -> p b g", b=TB)
        ssf = small[:, 32:40].rearrange("p (b g) -> p b g", b=TB)
        tot = small[:, 40:42]
        mpos = small[:, 42:44]

        gp = ctx.enter_context(nc.psum_tensor("gp", [P, 2, 2, NB], F32))
        mx = ctx.enter_context(nc.psum_tensor("mx", [P, 4, NB], F32))

        ext = nc.dram_tensor("ext", [H, EXT], F32, kind="Internal").ap()
        hankel = nc.dram_tensor("hankel", [H, P, T], F32, kind="Internal").ap()

        def sem(name):
            return ctx.enter_context(nc.semaphore(name))

        raw_in = [sem(f"raw_in{s}") for s in range(RING)]
        hi_ready = sem("hi_ready")
        lo_ready = sem("lo_ready")
        unit_used = sem("unit_used")
        bank_free = [sem(f"bank_free{i}") for i in range(2)]
        op_hi = sem("op_hi")
        op_ready = sem("op_ready")
        op_f32 = sem("op_f32")
        x_in = [sem(f"x_in{i}") for i in range(TB)]
        vec_in = sem("vec_in")
        rel_in = sem("rel_in")
        ext_made = sem("ext_made")
        ext_out = sem("ext_out")
        hankel_out = sem("hankel_out")
        consts = sem("consts")
        gp_self = sem("gp_self")
        ones_set = sem("ones_set")
        act_self = sem("act_self")
        dve_self = sem("dve_self")
        xn_ready = sem("xn_ready")
        turned = sem("turned")
        turned_out = sem("turned_out")
        vec_t = sem("vec_t")
        vec_ready = sem("vec_ready")
        lb_exp = sem("lb_exp")
        lb_max = sem("lb_max")
        sums = sem("sums")
        sums2 = sem("sums2")
        rstd_ready = sem("rstd_ready")
        evac_a = sem("evac_a")
        evac_v = sem("evac_v")
        sig_ready = sem("sig_ready")
        pre_ready = sem("pre_ready")
        ln_ready = sem("ln_ready")
        z_ready = sem("z_ready")
        e_ready = sem("e_ready")
        qk_ready = sem("qk_ready")
        prod_done = sem("prod_done")
        p_ready = sem("p_ready")
        cross_copied = sem("cross_copied")
        v_ready = sem("v_ready")
        head_ready = sem("head_ready")
        pv_done = sem("pv_done")
        o_copied = sem("o_copied")
        sq_ready = sem("sq_ready")
        ms_done = sem("ms_done")
        factors_used = sem("factors_used")
        qk_normed = sem("qk_normed")
        norm_part = sem("norm_part")
        hank_in = sem("hank_in")
        s_done = sem("s_done")
        max_done = sem("max_done")
        exp_done = sem("exp_done")
        pn_ready = sem("pn_ready")
        pt_done = sem("pt_done")
        pt_copied = sem("pt_copied")
        ws_in = sem("ws_in")
        bs_in = sem("bs_in")
        ws_turned = sem("ws_turned")
        ws_ready = sem("ws_ready")
        sv_done = sem("sv_done")
        sv_used = sem("sv_used")
        v_one_in = sem("v_one_in")
        y_f32 = sem("y_f32")
        fin_turned = sem("fin_turned")
        fin_copied = sem("fin_copied")
        gain_in = sem("gain_in")
        out_ready = sem("out_ready")
        out_done = sem("out_done")

        a_op, ff_op, y_op = (a_hi, a_lo), (ff_hi, ff_lo), (y_hi, y_lo)
        S = [
            Segment(w_in, "T", 2, D, (0, NB), 2 * NB, a_op),
            Segment(w_in, "N", 2, D, (2 * DM, 2 * DM + NB), 4 * DM, a_op),
            Segment(w_in, "T", 3, D, (3 * DM, 3 * DM + NB), 2 * NB, a_op),
            Segment(w_in, "T", 4, D, (7 * DM, 7 * DM + NB), 2 * NB, a_op),
            Segment(w_proj_a, "T", 2, DM, (0, NB), 2 * NB, a_op),
            Segment(w_proj_b, "T", 2, DM, (0, NB), 2 * NB, a_op, H),
            Segment(w_out, "T", 2, D, (0, NB), 2 * NB, a_op),
            Segment(w_ffn_in, "T", FF // NB, D, (0, FF), NB, a_op),
            Segment(w_ffn_out, "T", 2, FF, (0, NB), 2 * NB, ff_op),
            Segment(a_w_in, "N", 4, D, (E2, E2 + NB), 2 * NB, a_op),
            Segment(a_w_in, "T", G, D, (0, 2 * E2), NB, a_op),
            Segment(a_w_out, "N", 2, E2, (0, NB), 2 * NB, y_op),
        ]
        QF, IV, GQK, GATES, PROJ_A, PROJ_B, OUT, FFN_IN, FFN_OUT, V_IN, UG_IN, Y_OUT = range(len(S))
        unit0, block0 = [0], [0]
        for s in S:
            unit0.append(unit0[-1] + s.steps * s.pair)
            block0.append(block0[-1] + s.steps * 2)
        OPS = {QF: DT, PROJ_A: H + H, OUT: DT, FFN_IN: DT, FFN_OUT: FT, V_IN: DT, Y_OUT: ET}
        op0, n = {}, 0
        for k in range(len(S)):
            op0[k] = n
            n += OPS.get(k, 0)

        def after(k, i, units):
            return i * S[k].pair + (unit0[k] + units)

        block = ctx.enter_context(nc.Block())

        @block.sync
        def _(sp):
            for b in range(TB):
                sp.dma_start(x_tok[:, b], x[b * P:(b + 1) * P, :]).then_inc(x_in[b], 16)

            def load(k, i):
                s = S[k]
                for j in range(s.pair):
                    if (k, i) != (0, 0) or j >= RING:
                        sp.wait_ge(lo_ready, after(k, i, j + 1 - RING))
                    u = j % s.units
                    c = s.first[j // s.units]
                    src = s.w[u * UK * P:(u + 1) * UK * P, bass.ds(i * s.stride + c, NB)]
                    sp.dma_start(raw[:, j % RING], src.rearrange("(k p) n -> p k n", p=P)).then_inc(
                        raw_in[j % RING], 16)

            load(0, 0)
            with sp.Fori(1, S[0].steps) as i:
                load(0, i)
            for k in range(1, len(S)):
                with sp.Fori(0, S[k].steps) as i:
                    load(k, i)
            sp.wait_ge(unit_used, unit0[Y_OUT])
            sp.dma_start(gain_fin[:], final_norm.partition_broadcast(P)).then_inc(gain_in, 16)
            for b in range(TB):
                sp.wait_ge(out_ready, b + 1)
                sp.dma_start(out[b * P:(b + 1) * P, :], x_fin[:, b]).then_inc(out_done, 16)
            sp.wait_ge(out_done, 16 * TB)

        @block.gpsimd
        def _(pool):
            own = Chain(pool, gp_self)
            own.link(pool.memset(ident[:], 0.0))
            own.link(pool.memset(flip[:], 0.0))
            pool.affine_select(out=ident[:], in_=ident[:], compare_op=ALU.not_equal, fill=1.0, base=0,
                               pattern=[[-1, P]], channel_multiplier=1).then_inc(consts, 1)
            pool.affine_select(out=flip[:], in_=flip[:], compare_op=ALU.not_equal, fill=1.0,
                               base=1 - P, pattern=[[1, P]], channel_multiplier=1).then_inc(consts, 1)
            own.link(pool.memset(masks[:], 0.0))
            pool.affine_select(out=masks[:, 0], in_=masks[:, 0], compare_op=ALU.not_equal, fill=1.0,
                               base=0, pattern=[[-1, P]], channel_multiplier=1).then_inc(consts, 1)
            for l in range(MASKED - 1):
                w = 1 << l
                half = masks[:, 1 + l].rearrange("p (b h j) -> p b h j", h=2, j=w)[:, :, 1, :]
                own.link(pool.memset(half, 1.0))
                own.link(pool.affine_select(out=half, in_=half, compare_op=ALU.is_ge, fill=0.0, base=0,
                                            pattern=[[-2 * w, P // (2 * w)], [0, w]], channel_multiplier=1))
                pool.affine_select(out=half, in_=half, compare_op=ALU.is_ge, fill=0.0, base=w - 1,
                                   pattern=[[2 * w, P // (2 * w)], [0, w]],
                                   channel_multiplier=-1).then_inc(consts, 1)

            pool.wait_ge(ext_made, 1)
            pool.dma_start(ext, ext_sb).then_inc(ext_out, 16)
            pool.wait_ge(ext_out, 16)
            pool.dma_start(hankel, bass.AP(ext.tensor, 0, [[EXT, H], [1, P], [1, T]])).then_inc(hankel_out, 16)

            def weigh(h, buf):
                pool.wait_ge(e_ready, h + 1)
                pool.tensor_copy(key_head[buf][:], keys[:, bass.ds(h, 1)].rearrange("p a t -> p (a t)")).then_inc(head_ready, 1)
                for l in range(LEVELS):
                    w = 1 << l
                    two = decay[buf][:, l].rearrange("p (b h j) -> p b h j", h=2, j=w)
                    qh = q_a[:, bass.ds(h, 1)].rearrange("p a (b h j) -> p (a b) h j", h=2, j=w)
                    kh = keys[:, bass.ds(h, 1)].rearrange("p a (b h j) -> p (a b) h j", h=2, j=w)
                    pool.tensor_tensor(two[:, :, 1, :], two[:, :, 1, :], qh[:, :, 1, :], ALU.mult)
                    last = pool.tensor_tensor(two[:, :, 0, :], two[:, :, 0, :], kh[:, :, 0, :], ALU.mult)
                last.then_inc(qk_ready, 1)

            def head_values(h, which):
                pool.wait_ge(pv_done, h + (H * which + 1))
                pool.tensor_copy(v_head[:], val[:, which, :, bass.ds(h * DH, DH)]).then_inc(v_ready, 1)

            pool.wait_ge(pre_ready, 2)
            weigh(0, 0)
            pool.wait_ge(bank_free[1], 1 + block0[IV] // 2 + 1)
            head_values(0, 0)
            with pool.Fori(0, H // 2 - 1) as i:
                weigh(i * 2 + 1, 1)
                head_values(i * 2 + 1, 0)
                weigh(i * 2 + 2, 0)
                head_values(i * 2 + 2, 0)
            weigh(H - 1, 1)
            head_values(H - 1, 0)
            pool.wait_ge(qk_normed, 1)
            pool.wait_ge(hankel_out, 16)
            with pool.Fori(0, H) as h:
                pool.wait_ge(s_done, h + 1)
                pool.dma_start(hank[:], hankel[bass.ds(h, 1)].rearrange("a p t -> p (a t)")).then_inc(hank_in, 16)
                pool.tensor_copy(q_head[:], g_a[:, 1, bass.ds(h, 1)].rearrange("p a t -> p (a t)")).then_inc(head_ready, 1)
                head_values(h, 1)
            pool.wait_ge(op_ready, op0[V_IN] + DT)
            pool.dma_start(ws_raw[:], a_w_s.rearrange("g p q -> p g q")).then_inc(ws_in, 16)
            pool.wait_ge(sums, 1)
            pool.dma_start(bs_all[:].rearrange("p g n -> p (g n)"), a_b_s.partition_broadcast(P)).then_inc(bs_in, 16)
            with pool.Fori(0, G) as g:
                pool.wait_ge(sv_done, g + 1)
                pool.tensor_copy(v_one[:], v_g[:, bass.ds(g, 1)].rearrange("p a b n -> p (a b) n")).then_inc(v_one_in, 1)

        @block.scalar
        def _(act):
            own = Chain(act, act_self)

            def split(slot, use, used):
                act.wait_ge(raw_in[slot], use)
                if used is not None:
                    act.wait_ge(unit_used, used)
                act.activation(w_hi[:, slot], raw[:, slot], ACT.Copy).then_inc(hi_ready, 1)

            def step(k, i, evac, last=False, mid=None):
                s = S[k]
                for j in range(s.pair):
                    if not (last and j >= s.pair - RING):
                        n = unit0[k] + RING + j
                        split(j % RING, i * (16 * s.pair // RING) + 16 * (n // RING + 1),
                              after(k, i, j + 1))
                    if j % s.units == s.units - 1:
                        b = j // s.units
                        act.wait_ge(unit_used, after(k, i, j + 1))
                        evac(i, b)
                    if mid is not None:
                        mid(i, j)

            def run(k, evac, per=0, final=False, mid=None, begin=0, end=None):
                steps = (S[k].steps if end is None else end) - final
                if steps - begin == 1 and not final:
                    step(k, begin, evac, mid=mid)
                    return
                with act.Fori(begin, steps) as i:
                    own.enter(i - begin if begin else i, per)
                    step(k, i, evac, mid=mid)
                    own.leave(steps - begin)
                if final:
                    step(k, steps, evac, last=True)

            def none(i, b):
                pass

            rows = [(0, 0, norm_mix, 16), (0, 16, norm_ffn, 16), (0, 32, a_norm, 16), (0, 48, b_gate, 32),
                    (0, 80, a_v_gain, 32), (1, 0, lb_logits, 16), (1, 16, out_gain, 8), (1, 24, q_gain, 1),
                    (1, 25, k_gain, 1)]
            for which, r, src, n in rows:
                act.dma_start(vec_rows[r:r + n, which], src.rearrange("(r n) -> r n", n=P)).then_inc(vec_in, 16)
            act.dma_start(p_t[0:H, REL_FUTURE + 1:REL_FUTURE + 1 + N_REL], rel_bias).then_inc(rel_in, 16)
            act.wait_ge(ones_set, 1)
            for b in range(TB):
                act.wait_ge(x_in[b], 16)
                own.link(act.activation(wide4, x_tok[:, b], ACT.Square, accum_out=ssx[:, b:b + 1]))
            own.link(act.activation(rx, ssx, ACT.Ln, scale=1.0 / D, bias=eps_c))
            own.link(act.activation(rx, rx, ACT.Exp, scale=-0.5))
            for c in range(2):
                for b in range(TB):
                    if c:
                        act.wait_ge(turned, 4)
                    act.activation(wide4[:, b * D // 2:(b + 1) * D // 2], x_tok[:, b, c * D // 2:(c + 1) * D // 2],
                                   ACT.Copy, scale=rx[:, b:b + 1]).then_inc(xn_ready, 1)
                for g in range(4 * c, 4 * c + 4):
                    for m in (2 * g, 2 * g + 1):
                        if m == 2 * g:
                            act.wait_ge(turned, g + 1)
                            act.wait_ge(vec_ready, 1)
                        act.activation(a_hi[:, m], mx[:, g % 4, (m % 2) * T:(m % 2 + 1) * T], ACT.Copy,
                                       scale=col(GAIN_MIX + m)).then_inc(op_hi, 1)
            for n in range(RING):
                split(n, 16, None)
            for g in range(8):
                act.wait_ge(turned, 9 + g)
                act.activation(x_t[:, 2 * g:2 * g + 2].rearrange("p m t -> p (m t)"), mx[:, g % 4], ACT.Copy).then_inc(
                    turned_out, 1)
            act.wait_ge(lb_max, 1)
            act.activation(lbw[:, 2:4], lbw[:, 2:4], ACT.Exp).then_inc(lb_exp, 1)

            def copy_out(dst):
                def evac(i, b):
                    act.activation(dst(i, b), gp[:, b], ACT.Copy).then_inc(bank_free[b], 1)
                return evac

            act.sem_inc(o_copied, 1)
            act.sem_inc(exp_done, 1)
            run(QF, copy_out(lambda i, b: qf[:, bass.ds(i * 8 + 4 * b, 4)].rearrange("p (a c) t -> p a (c t)", a=2)))

            def copied(k):
                for b in range(2):
                    act.wait_ge(bank_free[b], 1 + block0[k + 1] // 2)

            def decay_exp(h, buf):
                act.wait_ge(z_ready, h + 1)
                act.activation(decay[buf][:], decay[buf][:], ACT.Exp).then_inc(e_ready, 1)

            def hgrn_first(i, j):
                if j == 0:
                    copied(QF)
                    act.activation(wide[:], q_a, ACT.Sigmoid).then_inc(sig_ready, 1)
                if j == 1:
                    act.activation(f_a, f_a, ACT.Sigmoid).then_inc(sig_ready, 1)
                if j == 4:
                    act.wait_ge(pre_ready, 1)
                    act.activation(f_a, f_a, ACT.Ln).then_inc(ln_ready, 1)
                if j == 11:
                    decay_exp(0, 0)

            val_out = copy_out(lambda i, b: val[:, bass.ds(i, 1), :, b * NB:(b + 1) * NB].rearrange("p a b n -> p (a b) n"))
            run(IV, val_out, mid=hgrn_first, end=1)
            run(IV, val_out, begin=1)

            def cross_copy(h):
                act.wait_ge(prod_done, h * 3 + 4)
                act.wait_ge(pv_done, h + 1)
                act.activation(p_t[:, P:2 * P], mx[:, 3, 0:P], ACT.Copy).then_inc(cross_copied, 1)

            def hgrn(i, j):
                h, u, b = i * 2 + j // 8, j % 8, j // 8
                if u == 2 and not (isinstance(i, int) and b == 1):
                    decay_exp(h + 1, 1 - b)
                if u == 4:
                    cross_copy(h)
                if u == 6:
                    act.wait_ge(pv_done, h + 2)
                    act.activation(q_a[:, bass.ds(h, 1)].rearrange("p a t -> p (a t)"), mx[:, 3, T:2 * T], ACT.Copy).then_inc(o_copied, 1)

            run(GQK, copy_out(lambda i, b: g_a[:, bass.ds(i, 1), 4 * b:4 * b + 4].rearrange("p a (b c) t -> p (a b) (c t)", c=2)), mid=hgrn)

            def rms(dst, src, dim):
                act.activation(dst, src, ACT.Sqrt, scale=1.0 / dim, bias=eps_c).then_inc(rstd_ready, 1)

            def gate_out(i, b):
                for m in range(4):
                    ins = act.activation(gates[:, bass.ds(i * 8 + (4 * b + m), 1)].rearrange("p a t -> p (a t)"),
                                         gp[:, b, m // 2, (m % 2) * T:(m % 2 + 1) * T], ACT.Sigmoid,
                                         bias=vec[:, 0, bass.ds(i * 8 + (B_GATE + 4 * b + m), 1)])
                ins.then_inc(bank_free[b], 1)

            def hgrn_end(i, j):
                hgrn(i + 3, j)

            def norms(i, j):
                for r, src in enumerate((q_a, q_b, k_b)):
                    if j == 5 * r:
                        copied(GQK)
                        act.wait_ge(o_copied, H + 1)
                        if r:
                            act.wait_ge(factors_used, r)
                        act.activation(wide[:], src, ACT.Square).then_inc(sq_ready, 1)
                    if j == 5 * r + 2:
                        act.wait_ge(ms_done, r + 1)
                        rms(wide4, mx[:].rearrange("p a n -> p (a n)"), DH)
                if j == 3:
                    act.activation(keys[:], g_a[:, 0], ACT.Sigmoid).then_inc(sig_ready, 1)

            def attention(i, j):
                h, u = (i - 2) * 4 + j // 4, j % 4
                if u == 0:
                    act.wait_ge(max_done, h + 1)
                    act.activation(p_n[:, 0:P], mx[:, 0, 0:P], ACT.Exp, bias=mneg[:, 0:1], accum_out=psum_[:, 0:1])
                    act.activation(p_n[:, P:3 * P], mx[:, 0, P:3 * P], ACT.Exp, bias=mneg[:, 1:2],
                                   accum_out=psum_[:, 1:2]).then_inc(exp_done, 1)
                if u == 2:
                    act.wait_ge(pt_done, h + 1)
                    act.activation(p_t[:], mx[:, 1, 0:3 * P], ACT.Copy).then_inc(pt_copied, 1)
                if u == 3:
                    act.wait_ge(pv_done, h + (H + 2))
                    act.activation(g_a[:, 1, bass.ds(h, 1)].rearrange("p a t -> p (a t)"), mx[:, 3, T:2 * T], ACT.Copy).then_inc(o_copied, 1)

            run(GATES, gate_out, mid=hgrn_end, end=1)
            run(GATES, gate_out, mid=norms, begin=1, end=2)
            run(GATES, gate_out, mid=attention, begin=2)
            act.wait_ge(unit_used, unit0[PROJ_A])
            act.wait_ge(y_f32, 1)
            for src, t in ((q_a, 0), (g_a[:, 1], H)):
                if t:
                    act.wait_ge(o_copied, 2 * H + 1)
                for c in range(2):
                    act.activation(a_hi[:, t + 4 * c:t + 4 * c + 4], src[:, 4 * c:4 * c + 4], ACT.Copy).then_inc(op_hi, 4)
            run(PROJ_A, none)
            run(PROJ_B, none)
            act.wait_ge(unit_used, unit0[OUT])
            for c in range(4):
                act.wait_ge(evac_v, c + 1)
                act.activation(a_hi[:, 4 * c:4 * c + 4], gates[:, 4 * c:4 * c + 4], ACT.Copy).then_inc(op_hi, 4)

            def residual(r):
                def evac(i, b):
                    act.wait_ge(evac_v, i * 2 + (5 + 4 * r + b))
                    act.activation(wide[:, 0:4], x_t[:, bass.ds(i * 8 + 4 * b, 4)], ACT.Square).then_inc(sq_ready, 1)
                return evac

            def next_operand(r, k):
                act.wait_ge(ms_done, 4 + r)
                rms(rstd[:], mx[:, 2, 0:T], D)
                act.wait_ge(unit_used, unit0[k])
                for c in range(4):
                    act.wait_ge(op_f32, 4 * r + c + 1)
                    act.activation(a_hi[:, 4 * c:4 * c + 4], wide[:, 4 * (c % 2):4 * (c % 2) + 4], ACT.Copy).then_inc(op_hi, 4)

            run(OUT, residual(0))
            next_operand(0, FFN_IN)

            def ffn(i, b):
                if b == 0:
                    act.wait_ge(op_ready, i * 4 + op0[FFN_OUT])
                    act.activation(wide[:, 0:4].rearrange("p (a c) t -> p a (c t)", a=2), gp[:, 0], ACT.Silu).then_inc(bank_free[0], 1)
                else:
                    act.wait_ge(y_f32, i + 2)
                    act.activation(ff_hi[:, bass.ds(i * 4, 4)], wide[:, 4:8], ACT.Copy).then_inc(op_hi, 4)

            run(FFN_IN, ffn)
            run(FFN_OUT, residual(1))
            next_operand(1, V_IN)

            act.wait_ge(op_ready, op0[V_IN] + DT)
            def v_out(i, b):
                for t in range(TB):
                    dst = v_g[:, bass.ds(i * 2 + b, 1), t].rearrange("p a n -> p (a n)")
                    own.link(act.activation(dst, gp[:, b, t], ACT.Gelu_apprx_tanh))
                for t in range(TB):
                    dst = v_g[:, bass.ds(i * 2 + b, 1), t].rearrange("p a n -> p (a n)")
                    ins = act.activation(wide4[:, t * NB:(t + 1) * NB], dst, ACT.Square,
                                         accum_out=ssv[:, t, bass.ds(i * 2 + b, 1)])
                own.link(ins)
                act.sem_inc(bank_free[b], 1)

            run(V_IN, v_out, per=6)
            act.sem_inc(sums, 1)
            act.wait_ge(sums2, 1)
            rms(rv, tot, E2)

            def ug(i, b):
                if b == 0:
                    act.wait_ge(y_f32, i + (1 + S[FFN_IN].steps))
                    act.activation(u_act[:].rearrange("p (a c) t -> p a (c t)", a=2), gp[:, 0], ACT.Gelu_apprx_tanh).then_inc(bank_free[0], 1)
                else:
                    act.activation(g_act[:].rearrange("p (a c) t -> p a (c t)", a=2), gp[:, 1], ACT.Silu).then_inc(bank_free[1], 1)
                    act.wait_ge(y_f32, i + (2 + S[FFN_IN].steps))
                    act.activation(y_hi[:, bass.ds(i * 4, 4)], y_one[:], ACT.Copy).then_inc(op_hi, 4)

            run(UG_IN, ug)
            for g in range(8):
                act.wait_ge(fin_turned, g + 1)
                b, c = g // 4, g % 4
                act.activation(x_fin[:, b, c * NB:(c + 1) * NB], mx[:, g % 4], ACT.Copy).then_inc(fin_copied, 1)

            def fin(i, b):
                for t in range(TB):
                    if t == 0:
                        act.wait_ge(evac_v, i * 2 + (13 + b))
                    own.link(act.activation(wide4[:, 0:NB], x_fin[:, t, bass.ds(i * 2 * NB + b * NB, NB)], ACT.Square,
                                            accum_out=ssf[:, t, bass.ds(i * 2 + b, 1)]))

            run(Y_OUT, fin, per=4, final=True)
            act.sem_inc(sums, 1)
            act.wait_ge(sums2, 2)
            rms(rf, tot, D)

        @block.vector
        def _(dve):
            own = Chain(dve, dve_self)

            def split(slot, n):
                dve.wait_ge(hi_ready, n)
                dve.tensor_tensor(w_lo[:, slot], raw[:, slot], w_hi[:, slot], ALU.subtract).then_inc(lo_ready, 1)

            def step(k, i, evac, last=False, mid=None):
                s = S[k]
                for j in range(s.pair):
                    if not (last and j >= s.pair - RING):
                        split(j % RING, after(k, i, RING + j + 1))
                    if j % s.units == s.units - 1:
                        b = j // s.units
                        dve.wait_ge(unit_used, after(k, i, j + 1))
                        evac(i, b)
                    if mid is not None:
                        mid(i, j)

            def run(k, evac, per=0, final=False, mid=None, begin=0, end=None):
                steps = (S[k].steps if end is None else end) - final
                if steps - begin == 1 and not final:
                    step(k, begin, evac, mid=mid)
                    return
                with dve.Fori(begin, steps) as i:
                    own.enter(i - begin if begin else i, per)
                    step(k, i, evac, mid=mid)
                    own.leave(steps - begin)
                if final:
                    step(k, steps, evac, last=True)

            def none(i, b):
                pass

            dve.memset(small[:, 0:1], EPS)
            dve.memset(gp[:, 0, 0, 0:1], 0.0).then_inc(bank_free[0], 1)
            dve.memset(gp[:, 1, 0, 0:1], 0.0).then_inc(bank_free[1], 1)
            dve.memset(ones[:], 1.0).then_inc(ones_set, 1)
            dve.wait_ge(rel_in, 16)
            dve.tensor_copy(ext_sb[:, 0:REL_FUTURE + 1], ext_sb[:, REL_FUTURE + 1:REL_FUTURE + 2].broadcast_to([H, REL_FUTURE + 1]))
            e = REL_FUTURE + 1 + N_REL
            dve.tensor_copy(ext_sb[:, e:EXT], ext_sb[:, e - 1:e].broadcast_to([H, EXT - e])).then_inc(ext_made, 1)
            dve.wait_ge(vec_t, 1)
            own.link(dve.tensor_copy(vec[:, 0, 0:ROWS0], mx[:, 0, 0:ROWS0]))
            own.link(dve.tensor_copy(vec[:, 1, 0:ROWS1], mx[:, 1, 0:ROWS1]))
            dve.tensor_scalar(gq_c, vec[:, 1, Q_GAIN:Q_GAIN + 1], DH ** -0.5, None, ALU.mult).then_inc(vec_ready, 1)
            for g in range(8):
                for m in (2 * g, 2 * g + 1):
                    dve.wait_ge(op_hi, 2 * g + 2)
                    dve.scalar_tensor_tensor(out=a_lo[:, m], in0=mx[:, g % 4, (m % 2) * T:(m % 2 + 1) * T],
                                             scalar=col(GAIN_MIX + m), in1=a_hi[:, m].bitcast(F32), op0=ALU.mult,
                                             op1=ALU.subtract).then_inc(op_ready, 1)
            for n in range(RING):
                split(n, n + 1)
            l0, l1 = vec[:, 1, LB0:LB0 + H], vec[:, 1, LB1:LB1 + H]
            own.link(dve.tensor_tensor(lbw[:, 0], l0, l1, ALU.max))
            dve.tensor_tensor(lbw[:, 2], l0, lbw[:, 0], ALU.subtract)
            dve.tensor_tensor(lbw[:, 3], l1, lbw[:, 0], ALU.subtract).then_inc(lb_max, 1)
            dve.wait_ge(lb_exp, 1)
            own.link(dve.tensor_tensor(lbw[:, 0], lbw[:, 2], lbw[:, 3], ALU.add))
            own.link(dve.reciprocal(lbw[:, 1], lbw[:, 0]))
            own.link(dve.tensor_tensor(lbw[:, 4], lbw[:, 2], lbw[:, 1], ALU.mult))
            own.link(dve.tensor_scalar(lbw[:, 5], lbw[:, 4], -1.0, 1.0, ALU.mult, ALU.add))

            dve.sem_inc(p_ready, 1)
            dve.sem_inc(sv_used, 1)
            run(QF, none)

            def decays(h, buf, part_):
                out_ = decay[buf]
                if part_ == 0:
                    sums_within(h)
                for l in range(4 * part_, 4 * part_ + 4 - part_):
                    w = 1 << l
                    b4 = scan[:].rearrange("p (b h j) -> p b h j", h=2, j=w)
                    z4 = out_[:, l].rearrange("p (b h j) -> p b h j", h=2, j=w)
                    ref = b4[:, :, 0, w - 1:w].broadcast_to([P, T // (2 * w), w])
                    if w < CHUNK:
                        dve.tensor_tensor(z4[:, :, 1, :], b4[:, :, 1, :], ref, ALU.subtract)
                    else:
                        dve.tensor_copy(z4[:, :, 1, :], b4[:, :, 1, :])
                    dve.tensor_tensor(z4[:, :, 0, :], ref, b4[:, :, 0, :], ALU.subtract)
                if part_ == 1:
                    z, c1, c2, c3 = out_[:, LEVELS - 1], CHUNK, 2 * CHUNK, 3 * CHUNK
                    dve.tensor_scalar(z[:, c1:c2], scan[:, c1:c2], scan[:, c2 - 1:c2], -1.0, ALU.subtract, ALU.mult)
                    dve.tensor_copy(z[:, c2:c3], scan[:, c2:c3])
                    dve.tensor_scalar(z[:, c3:T], scan[:, c3:T], scan[:, c3 - 1:c3], None, ALU.add)
                    own.link(dve.tensor_scalar(z[:, 0:c1], scan[:, 0:c1], scan[:, c1 - 1:c1], -1.0, ALU.subtract, ALU.mult))
                    dve.tensor_scalar(z[:, 0:c1], z[:, 0:c1], scan[:, c2 - 1:c2], None, ALU.add).then_inc(z_ready, 1)

            def sums_within(h):
                lf = f_a[:, bass.ds(h, 1)].rearrange("p a t -> p (a t)")
                for c in range(T // CHUNK):
                    c0, c1 = c * CHUNK, (c + 1) * CHUNK
                    ins = dve.tensor_tensor_scan(scan[:, c0:c1], ones[:, 0:CHUNK], lf[:, c0:c1], 0.0, ALU.mult, ALU.add)
                own.link(ins)

            def scores(h, b):
                dve.wait_ge(prod_done, h * 3 + (b + 2))
                dve.wait_ge(pv_done, h + 1)
                part8 = mx[:, 0:2].rearrange("p a n -> p (a n)")
                own.link(dve.tensor_tensor(masked[:].rearrange("p l t -> p (l t)"), part8[:, 0:MASKED * P],
                                           masks[:].rearrange("p l t -> p (l t)"), ALU.mult))
                dst = p_t[:, 2 * b * P:(2 * b + 1) * P]
                own.link(dve.tensor_reduce(dst, masked[:].rearrange("p l t -> p t l"), AX_X, ALU.add))
                dve.tensor_tensor(dst[0:CHUNK, CHUNK:P], dst[0:CHUNK, CHUNK:P],
                                  part8[0:CHUNK, MASKED * P:MASKED * P + CHUNK], ALU.add).then_inc(p_ready, 1)

            def hgrn_first(i, j):
                if j == 1:
                    dve.wait_ge(sig_ready, 2)
                    for h in range(H):
                        ins = dve.tensor_scalar(f_a[:, h], f_a[:, h], lbw[:, 5, h:h + 1], lbw[:, 4, h:h + 1], ALU.mult, ALU.add)
                    own.link(ins)
                if j == 2:
                    own.link(dve.tensor_scalar(keys[:], f_a, -1.0, 1.0, ALU.mult, ALU.add))
                if j == 3:
                    dve.tensor_scalar(f_a, f_a, LN_MIN, None, ALU.max).then_inc(pre_ready, 1)
                if j == 5:
                    dve.tensor_tensor(q_a, q_a, wide[:], ALU.mult).then_inc(pre_ready, 1)
                    dve.wait_ge(consts, 2 + MASKED)
                    dve.wait_ge(ln_ready, 1)
                    dve.wait_ge(pre_ready, 2)
                if j in (7, 8):
                    decays(0, 0, j - 7)

            run(IV, none, mid=hgrn_first, end=1)
            run(IV, none, begin=1)

            def hgrn(i, j):
                h, u, b = i * 2 + j // 8, j % 8, j // 8
                if u in (0, 1) and not (isinstance(i, int) and b == 1):
                    if u == 0:
                        dve.wait_ge(prod_done, h * 3 + 1)
                    decays(h + 1, 1 - b, u)
                if u in (2, 4):
                    scores(h, u // 2 - 1)

            run(GQK, none, per=12, mid=hgrn)

            def hgrn_end(i, j):
                hgrn(i + 3, j)

            def norms(i, j):
                flat = lambda a: a.rearrange("p h t -> p (h t)")
                for r in range(3):
                    if j == 5 * r + 3:
                        dve.wait_ge(rstd_ready, r + 1)
                        own.link(dve.reciprocal(wide[:], wide[:]))
                if j == 4:
                    for h in range(H):
                        ins = dve.scalar_tensor_tensor(out=q_a[:, h], in0=q_a[:, h], scalar=vec[:, 1, OUT_GAIN + h:OUT_GAIN + h + 1],
                                                       in1=wide[:, h], op0=ALU.mult, op1=ALU.mult)
                    ins.then_inc(factors_used, 1)
                if j == 6:
                    dve.wait_ge(sig_ready, 3)
                    own.link(dve.tensor_tensor(keys[:], keys[:], g_a[:, 0], ALU.mult))
                if j == 7:
                    dve.wait_ge(factors_used, 1)
                    dve.tensor_tensor(q_a, q_a, keys[:], ALU.mult).then_inc(y_f32, 1)
                if j == 9:
                    dve.scalar_tensor_tensor(out=flat(q_b), in0=flat(q_b), scalar=gq_c, in1=wide4, op0=ALU.mult,
                                             op1=ALU.mult).then_inc(factors_used, 1)
                if j == 14:
                    dve.scalar_tensor_tensor(out=flat(k_b), in0=flat(k_b), scalar=vec[:, 1, K_GAIN:K_GAIN + 1],
                                             in1=wide4, op0=ALU.mult, op1=ALU.mult).then_inc(qk_normed, 1)

            def attention(i, j):
                h, u = (i - 2) * 4 + j // 4, j % 4
                if u == 0:
                    dve.wait_ge(s_done, h + 2)
                    s3 = mx[:, 0, 0:3 * P]
                    hidden = mx[0:CHUNK, 0, 0:3 * P].rearrange("p (a n) -> p a n", n=P)[:, 0:3:2, CHUNK:P]
                    own.link(dve.memset(hidden, NEG))
                    dve.tensor_reduce(mpos[:, 0:1], s3[:, 0:P], AX_X, ALU.max)
                    own.link(dve.tensor_reduce(mpos[:, 1:2], s3[:, P:3 * P], AX_X, ALU.max))
                    dve.tensor_scalar(mneg, mpos, -1.0, None, ALU.mult).then_inc(max_done, 1)
                if u == 1:
                    dve.wait_ge(exp_done, h + 2)
                    own.link(dve.reciprocal(rsum, psum_))
                    dve.tensor_scalar(p_n[:, 0:P], p_n[:, 0:P], rsum[:, 0:1], None, ALU.mult)
                    dve.tensor_scalar(p_n[:, P:3 * P], p_n[:, P:3 * P], rsum[:, 1:2], None, ALU.mult).then_inc(pn_ready, 1)

            run(GATES, none, mid=hgrn_end, end=1)
            run(GATES, none, mid=norms, begin=1, end=2)
            run(GATES, none, per=12, mid=attention, begin=2)
            dve.wait_ge(o_copied, 2 * H + 1)
            for src, t in ((q_a, 0), (g_a[:, 1], H)):
                for c in range(2):
                    t0 = t + 4 * c
                    dve.wait_ge(op_hi, op0[PROJ_A] + t0 + 4)
                    dve.tensor_tensor(a_lo[:, t0:t0 + 4], src[:, 4 * c:4 * c + 4], a_hi[:, t0:t0 + 4].bitcast(F32),
                                      ALU.subtract).then_inc(op_ready, 4)

            def proj_a(i, b):
                g4 = gates[:, bass.ds(i * 8 + 4 * b, 4)].rearrange("p (a c) t -> p a (c t)", a=2)
                dve.tensor_tensor(g4, gp[:, b], g4, ALU.mult).then_inc(bank_free[b], 1)

            def proj_b(i, b):
                ga = gates[:, bass.ds(i * 8 + 4 * b, 4)].rearrange("p (a c) t -> p a (c t)", a=2)
                gb = gates[:, bass.ds(i * 8 + (DT + 4 * b), 4)].rearrange("p (a c) t -> p a (c t)", a=2)
                own.link(dve.tensor_tensor(gb, gp[:, b], gb, ALU.mult))
                dve.sem_inc(bank_free[b], 1)
                dve.tensor_tensor(ga, ga, gb, ALU.add).then_inc(evac_v, 1)

            run(PROJ_A, proj_a)
            run(PROJ_B, proj_b, per=2)
            for c in range(4):
                dve.wait_ge(op_hi, op0[OUT] + 4 * c + 4)
                dve.tensor_tensor(a_lo[:, 4 * c:4 * c + 4], gates[:, 4 * c:4 * c + 4],
                                  a_hi[:, 4 * c:4 * c + 4].bitcast(F32), ALU.subtract).then_inc(op_ready, 4)

            def residual(r):
                def evac(i, b):
                    x4 = x_t[:, bass.ds(i * 8 + 4 * b, 4)].rearrange("p (a c) t -> p a (c t)", a=2)
                    own.link(dve.tensor_tensor(x4, gp[:, b], x4, ALU.add))
                    dve.sem_inc(evac_v, 1)
                    dve.sem_inc(bank_free[b], 1)
                    dve.wait_ge(sq_ready, i * 2 + (4 + 4 * r + b))
                    own.link(dve.tensor_reduce(part[:], wide[:, 0:4].rearrange("p m t -> p t m"), AX_X, ALU.add))
                    own.link(dve.tensor_tensor(total[:], total[:], part[:], ALU.add))
                return evac

            def next_operand(r, gain, k):
                dve.wait_ge(rstd_ready, 4 + r)
                own.link(dve.reciprocal(rstd[:], rstd[:]))
                for c in range(4):
                    if c >= 2:
                        dve.wait_ge(op_ready, op0[k] + 4 * (c - 1))
                    for m in range(4 * c, 4 * c + 4):
                        ins = dve.scalar_tensor_tensor(out=wide[:, m % 8], in0=x_t[:, m], scalar=col(gain + m),
                                                       in1=rstd[:], op0=ALU.mult, op1=ALU.mult)
                    ins.then_inc(op_f32, 1)
                    dve.wait_ge(op_hi, op0[k] + 4 * c + 4)
                    dve.tensor_tensor(a_lo[:, 4 * c:4 * c + 4], wide[:, 4 * (c % 2):4 * (c % 2) + 4],
                                      a_hi[:, 4 * c:4 * c + 4].bitcast(F32), ALU.subtract).then_inc(op_ready, 4)

            own.link(dve.memset(total[:], 0.0))
            run(OUT, residual(0), per=6)
            dve.sem_inc(norm_part, 1)
            next_operand(0, GAIN_FFN, FFN_IN)

            def ffn(i, b):
                if b == 0:
                    return
                dve.wait_ge(bank_free[0], i + (block0[FFN_IN] // 2 + 2))
                up = wide[:, 4:8].rearrange("p (a c) t -> p a (c t)", a=2)
                own.link(dve.tensor_tensor(up, gp[:, 1], wide[:, 0:4].rearrange("p (a c) t -> p a (c t)", a=2), ALU.mult))
                dve.sem_inc(bank_free[1], 1)
                dve.sem_inc(y_f32, 1)
                dve.wait_ge(op_hi, i * 4 + (op0[FFN_OUT] + 4))
                dve.tensor_tensor(ff_lo[:, bass.ds(i * 4, 4)], wide[:, 4:8], ff_hi[:, bass.ds(i * 4, 4)].bitcast(F32),
                                  ALU.subtract).then_inc(op_ready, 4)

            run(FFN_IN, ffn, per=1)
            own.link(dve.memset(total[:], 0.0))
            run(FFN_OUT, residual(1), per=6)
            dve.sem_inc(norm_part, 1)
            next_operand(1, GAIN_A, V_IN)

            run(V_IN, none)
            dve.wait_ge(sums, 1)
            own.link(dve.tensor_reduce(tot, ssv, AX_X, ALU.add))
            dve.sem_inc(sums2, 1)
            dve.wait_ge(rstd_ready, 6)
            own.link(dve.reciprocal(rv, rv))
            dve.wait_ge(ws_turned, 1)
            dve.wait_ge(bs_in, 16)
            for t in range(TB):
                ins = dve.tensor_scalar(ws_t[:, t].rearrange("p g n -> p (g n)"),
                                        mx[:, 0:2].rearrange("p a n -> p (a n)"), rv[:, t:t + 1], None, ALU.mult)
            ins.then_inc(ws_ready, 1)

            def ug(i, b):
                if b == 0:
                    dve.wait_ge(sv_done, i + 2)
                    dve.wait_ge(op_hi, i * 4 + op0[Y_OUT])
                    for c in range(4):
                        ins = dve.scalar_tensor_tensor(
                            out=y_one[:, c].rearrange("p (b t) -> p b t", b=TB),
                            in0=mx[:, c // 2, (c % 2) * T:(c % 2 + 1) * T].rearrange("p (b t) -> p b t", b=TB),
                            scalar=vec[:, 0, bass.ds(i * 4 + (V_GAIN + c), 1)],
                            in1=bs_all[:, bass.ds(i, 1)].broadcast_to([P, TB, P]), op0=ALU.mult, op1=ALU.add)
                    own.link(ins)
                    dve.sem_inc(sv_used, 1)
                    dve.wait_ge(bank_free[0], i + (block0[UG_IN] // 2 + 2))
                    own.link(dve.tensor_tensor(y_one[:], y_one[:], u_act[:], ALU.mult))
                else:
                    dve.wait_ge(bank_free[1], i + (block0[UG_IN] // 2 + 2))
                    own.link(dve.tensor_tensor(y_one[:], y_one[:], g_act[:], ALU.mult))
                    dve.sem_inc(y_f32, 1)
                    dve.wait_ge(op_hi, i * 4 + (op0[Y_OUT] + 4))
                    dve.tensor_tensor(y_lo[:, bass.ds(i * 4, 4)], y_one[:], y_hi[:, bass.ds(i * 4, 4)].bitcast(F32),
                                      ALU.subtract).then_inc(op_ready, 4)

            run(UG_IN, ug, per=3)

            def fin(i, b):
                if not isinstance(i, int) and b == 0:
                    dve.wait_ge(fin_copied, 8)
                xf = x_fin[:, :, bass.ds(i * 2 * NB + b * NB, NB)]
                own.link(dve.tensor_tensor(xf, gp[:, b], xf, ALU.add))
                dve.sem_inc(evac_v, 1)
                dve.sem_inc(bank_free[b], 1)

            run(Y_OUT, fin, per=2, final=True)
            dve.wait_ge(sums, 2)
            own.link(dve.tensor_reduce(tot, ssf, AX_X, ALU.add))
            dve.sem_inc(sums2, 1)
            dve.wait_ge(rstd_ready, 7)
            own.link(dve.reciprocal(rf, rf))
            dve.wait_ge(gain_in, 16)
            for b in range(TB):
                dve.scalar_tensor_tensor(out=x_fin[:, b], in0=x_fin[:, b], scalar=rf[:, b:b + 1], in1=gain_fin[:],
                                         op0=ALU.mult, op1=ALU.mult).then_inc(out_ready, 1)

        @block.tensor
        def _(pe):
            def unit(k, i, j):
                s = S[k]
                hi, lo = s.operand
                b, u, slot = j // s.units, j % s.units, j % RING
                pe.wait_ge(lo_ready, after(k, i, j + 1))
                for kk in range(UK):
                    t = s.tile0 + u * UK + kk
                    first = u == 0 and kk == 0
                    last = u == s.units - 1 and kk == UK - 1
                    for m in range(4 if s.form == "T" else 2):
                        for p, (wp, ap) in enumerate(((w_hi, hi), (w_hi, lo), (w_lo, hi))):
                            if s.form == "T":
                                out_ = gp[:, b, m // 2, (m % 2) * T:(m % 2 + 1) * T]
                                stat, mov = wp[:, slot, kk, m * P:(m + 1) * P], ap[:, t, :]
                                start = first and m % 2 == 0 and p == 0
                            else:
                                out_ = gp[:, b, m, :]
                                stat, mov = ap[:, t, m * P:(m + 1) * P], wp[:, slot, kk, :]
                                start = first and p == 0
                            ins = pe.matmul(out_, stat, mov, start=start, stop=last and p == 2, skip_group_check=True)
                ins.then_inc(unit_used, 1)

            def step(k, i, operand, mid):
                s = S[k]
                for j in range(s.pair):
                    if j % s.units == 0:
                        b = j // s.units
                        pe.wait_ge(bank_free[b], i + (block0[k] // 2 + 1))
                    if operand is not None:
                        pe.wait_ge(op_ready, operand + min(s.tile0 % DT + (j % s.units + 1) * UK, OPS_MAX[k]))
                    unit(k, i, j)
                    if mid is not None:
                        mid(i, j)

            def run(k, operand=None, mid=None, begin=0, end=None):
                end = S[k].steps if end is None else end
                if end - begin == 1:
                    step(k, begin, operand, mid)
                    return
                with pe.Fori(begin, end) as i:
                    step(k, i, operand, mid)

            OPS_MAX = {QF: DT, PROJ_A: H, PROJ_B: 2 * H, OUT: DT, FFN_IN: DT, V_IN: DT}

            pe.wait_ge(consts, 2)
            pe.wait_ge(vec_in, 16 * 9)
            pe.transpose(mx[:, 0, 0:ROWS0], vec_rows[0:ROWS0, 0], ident[0:ROWS0, 0:ROWS0])
            pe.transpose(mx[:, 1, 0:ROWS1], vec_rows[0:ROWS1, 1], ident[0:ROWS1, 0:ROWS1]).then_inc(vec_t, 1)
            pe.wait_ge(vec_ready, 1)
            for g in range(8):
                if g >= 4:
                    pe.wait_ge(op_ready, 2 * (g - 3))
                pe.wait_ge(xn_ready, 2 * (g // 4) + 2)
                for m in (2 * g, 2 * g + 1):
                    for b in range(TB):
                        c0 = b * D // 2 + (m % 8) * P
                        ins = pe.transpose(mx[:, g % 4, (m % 2) * T + b * P:(m % 2) * T + (b + 1) * P],
                                           wide4[:, c0:c0 + P], ident[:])
                ins.then_inc(turned, 1)
            for g in range(8):
                pe.wait_ge(op_ready, min(2 * (g + 5), 16))
                if g >= 4:
                    pe.wait_ge(turned_out, g - 3)
                for m in (2 * g, 2 * g + 1):
                    for b in range(TB):
                        ins = pe.transpose(mx[:, g % 4, (m % 2) * T + b * P:(m % 2) * T + (b + 1) * P],
                                           x_tok[:, b, m * P:(m + 1) * P], ident[:])
                ins.then_inc(turned, 1)

            for credit in (prod_done, pv_done, s_done, sv_done):
                pe.sem_inc(credit, 1)
            run(QF, op0[QF])
            run(IV)

            def level_products(h, b, buf):
                tb = slice(b * P, (b + 1) * P)
                if b == 0:
                    pe.wait_ge(qk_ready, h + 1)
                pe.wait_ge(p_ready, h * 2 + (b + 1))
                part8 = mx[:, 0:2].rearrange("p a n -> p (a n)")
                pe.matmul(part8[:, 0:P], key_head[buf][:, tb], q_a[:, bass.ds(h, 1), tb].rearrange("p a t -> p (a t)"),
                          start=True, stop=True, skip_group_check=True)
                for l in range(MASKED - 1):
                    pe.matmul(part8[:, (l + 1) * P:(l + 2) * P], decay[buf][:, l, tb], decay[buf][:, l, tb],
                              start=True, stop=True, skip_group_check=True)
                c0 = b * P
                pe.matmul(part8[0:CHUNK, MASKED * P:MASKED * P + CHUNK], decay[buf][:, LEVELS - 2, c0:c0 + CHUNK],
                          decay[buf][:, LEVELS - 2, c0 + CHUNK:c0 + P], start=True, stop=True,
                          skip_group_check=True).then_inc(prod_done, 1)

            def values(h):
                pe.wait_ge(v_ready, h + 1)
                pe.wait_ge(o_copied, h + 1)
                pe.matmul(mx[:, 3, T:2 * T], v_head[:, 0], p_t[:, 0:T], start=True, stop=False, skip_group_check=True)
                pe.matmul(mx[:, 3, T + P:2 * T], v_head[:, 1], p_t[:, T:3 * P], start=False, stop=True,
                          skip_group_check=True).then_inc(pv_done, 1)

            def hgrn(i, j):
                h, u, b = i * 2 + j // 8, j % 8, j // 8
                if u == 1:
                    level_products(h, 0, b)
                if u == 3:
                    level_products(h, 1, b)
                    pe.wait_ge(o_copied, h + 1)
                    pe.matmul(mx[:, 3, 0:P], decay[b][:, LEVELS - 1, 0:P], decay[b][:, LEVELS - 1, P:T], start=True,
                              stop=True, skip_group_check=True).then_inc(prod_done, 1)
                if u == 6:
                    pe.wait_ge(p_ready, h * 2 + 3)
                    pe.wait_ge(cross_copied, h + 1)
                    values(h)

            run(GQK, mid=hgrn)

            def hgrn_end(i, j):
                hgrn(i + 3, j)

            def norms(i, j):
                for r in range(3):
                    if j == 5 * r + 1:
                        pe.wait_ge(sq_ready, r + 1)
                        pe.wait_ge(o_copied, H + 1)
                        for b in range(4):
                            ins = pe.matmul(mx[:, b], ones[:], wide4[:, b * NB:(b + 1) * NB], start=True, stop=True,
                                            skip_group_check=True)
                        ins.then_inc(ms_done, 1)

            def attention(i, j):
                h, u = (i - 2) * 4 + j // 4, j % 4
                if u == 0:
                    if j == 0:
                        pe.wait_ge(qk_normed, 1)
                    pe.wait_ge(hank_in, h * 16 + 16)
                    pe.wait_ge(head_ready, h + (H + 1))
                    pe.wait_ge(exp_done, h + 1)
                    kh = g_a[:, 2, bass.ds(h, 1)].rearrange("p a t -> p (a t)")
                    s_ = mx[:, 0]
                    pe.matmul(s_[:, 0:P], hank[:, 0:P], flip[:], start=True, stop=False, skip_group_check=True)
                    pe.matmul(s_[:, P:2 * P], hank[:, P:T], flip[:], start=False, stop=False, skip_group_check=True)
                    pe.matmul(s_[:, 2 * P:3 * P], hank[:, 0:P], flip[:], start=False, stop=False, skip_group_check=True)
                    pe.matmul(s_[:, 0:P], q_head[:, 0:P], kh[:, 0:P], start=False, stop=True, skip_group_check=True)
                    pe.matmul(s_[:, P:3 * P], q_head[:, P:T], kh, start=False, stop=True,
                              skip_group_check=True).then_inc(s_done, 1)
                if u == 2:
                    pe.wait_ge(pn_ready, h + 1)
                    for c in range(3):
                        ins = pe.transpose(mx[:, 1, c * P:(c + 1) * P], p_n[:, c * P:(c + 1) * P], ident[:])
                    ins.then_inc(pt_done, 1)
                if u == 3:
                    pe.wait_ge(pt_copied, h + 1)
                    values(h + H)

            run(GATES, mid=hgrn_end, end=1)
            run(GATES, mid=norms, begin=1, end=2)
            run(GATES, mid=attention, begin=2)
            run(PROJ_A, op0[PROJ_A])
            run(PROJ_B, op0[PROJ_A])

            def norm_sum(r):
                pe.wait_ge(norm_part, r + 1)
                pe.matmul(mx[:, 2, 0:T], ones[:], total[:], start=True, stop=True).then_inc(ms_done, 1)

            run(OUT, op0[OUT])
            norm_sum(0)
            run(FFN_IN, op0[FFN_IN])
            pe.wait_ge(op_ready, op0[FFN_OUT] + FT)
            run(FFN_OUT)
            norm_sum(1)
            run(V_IN, op0[V_IN])
            pe.wait_ge(ws_in, 16)
            for g in range(G):
                ins = pe.transpose(mx[:, g // 4, (g % 4) * P:(g % 4 + 1) * P], ws_raw[:, g], ident[:])
            ins.then_inc(ws_turned, 1)
            pe.wait_ge(ws_ready, 1)

            def mix(g, j):
                if j != 2:
                    return
                pe.wait_ge(v_one_in, g + 1)
                pe.wait_ge(sv_used, g + 1)
                for c in range(4):
                    for b in range(TB):
                        t0 = (c % 2) * T + b * P
                        ins = pe.matmul(mx[:, c // 2, t0:t0 + P], v_one[:, b, c * P:(c + 1) * P],
                                        ws_t[:, b, bass.ds(g, 1)].rearrange("p a n -> p (a n)"),
                                        start=True, stop=True, skip_group_check=True)
                ins.then_inc(sv_done, 1)

            run(UG_IN, mid=mix)
            for g in range(8):
                if g >= 4:
                    pe.wait_ge(fin_copied, g - 3)
                if g == 0:
                    pe.wait_ge(sv_used, G + 1)
                b, c = g // 4, g % 4
                for m in range(4):
                    ins = pe.transpose(mx[:, g % 4, m * P:(m + 1) * P], x_t[:, 4 * c + m, b * P:(b + 1) * P], ident[:])
                ins.then_inc(fin_turned, 1)
            pe.wait_ge(op_ready, op0[Y_OUT] + ET)
            run(Y_OUT)


def kernel(**inputs):
    import numpy as np
    import concourse.bacc as bacc
    from concourse.bass_utils import run_bass_kernel_spmd

    nc = bacc.Bacc("TRN2", target_bir_lowering=False, num_devices=1)
    arrays = {}

    def given(name):
        a = np.ascontiguousarray(inputs[name])
        arrays[name + "_in"] = a
        return nc.dram_tensor(name + "_in", a.shape, F32, kind="ExternalInput").ap()

    one = lambda name: given(name)[0]
    out = nc.dram_tensor("result", [1, T, D], F32, kind="ExternalOutput").ap()
    build(nc, one("x"), one("w_in"), one("b_gate"), one("norm_mix"), one("norm_ffn"),
          given("hgrn_lb_logits").rearrange("a n -> (a n)"), one("hgrn_out_gain"), one("q_gain"), one("k_gain"),
          one("rel_bias"), one("w_proj_a"), one("w_proj_b"), one("w_out"), one("w_ffn_in"), one("w_ffn_out"),
          one("a_norm_2"), one("a_w_in_2"), one("a_v_gain_2"), one("a_w_s_2"),
          one("a_b_s_2").rearrange("g n -> (g n)"), one("a_w_out_2"), given("final_norm_2"), out[0])
    got = run_bass_kernel_spmd(nc, [arrays], core_ids=[0])
    return got.results[0]["result"]
```

```python
from contextlib import ExitStack

import concourse.bass as bass
from concourse import mybir

ALU = mybir.AluOpType
ACT = mybir.ActivationFunctionType
F32 = mybir.dt.float32
F32R = mybir.dt.float32r
AX_X = mybir.AxisListType.X

P = 128
T = 256
TB = T // P
D = 2048
DT = D // P
H = 8
DH = 128
DM = H * DH
CHUNK = 64
N_REL = 191
REL_FUTURE = CHUNK - 1
FF = 5632
FT = FF // P
E2 = 4096
ET = E2 // P
G = 8
EPS = 1e-6
NEG = -3.0e38
LN_MIN = 2.0 ** -64

NB = 512
UK = 2
RING = 4
LEVELS = 8
MASKED = 7
EXT = 384


class Segment:

    def __init__(self, weights, form, steps, rows, first, stride, operand):
        self.w, self.form, self.steps, self.units = weights, form, steps, rows // (UK * P)
        self.first, self.stride = first, stride
        self.operand = operand
        self.pair = 2 * self.units
        assert self.pair % RING == 0


class Chain:

    def __init__(self, eng, sem):
        self.eng, self.sem, self.base, self.step, self.at = eng, sem, 0, 0, 0

    def value(self):
        return self.at + self.base if not self.step else self.step[0] * self.step[1] + (self.base + self.at)

    def link(self, instruction):
        instruction.then_inc(self.sem, 1)
        self.at += 1
        self.eng.wait_ge(self.sem, self.value())

    def enter(self, i, per):
        self.base, self.at, self.step = self.base + self.at, 0, (i, per)

    def leave(self, steps):
        assert self.at == self.step[1], (self.at, self.step[1])
        self.base, self.at, self.step = self.base + steps * self.step[1], 0, 0


def build(nc, x, w_in, b_gate, norm_mix, norm_ffn, lb_logits, out_gain, q_gain, k_gain, rel_bias,
          w_proj_a, w_proj_b, w_out, w_ffn_in, w_ffn_out, a_norm, a_w_in, a_v_gain, a_w_s, a_b_s,
          a_w_out, final_norm, out):
    ctx = ExitStack()
    with ctx:
        top = [(nc.sbuf_base + 63) // 64 * 64]

        def at(name, shape, offset, dt=F32):
            return nc.alloc_sbuf_tensor_at(name, [P] + shape, dt, offset=offset)

        def size(shape):
            n = 4
            for s in shape:
                n *= s
            return n

        def new(name, shape, dt=F32):
            offset = top[0]
            top[0] += (size(shape) + 31) // 32 * 32
            return at(name, shape, offset, dt)

        raw = new("raw", [RING, UK, NB])
        w_hi = new("w_hi", [RING, UK, NB], F32R)
        w_lo = new("w_lo", [RING, UK, NB], F32R)
        a_at = top[0]
        a_hi = new("a_hi", [DT, T], F32R)
        a_lo = new("a_lo", [DT, T], F32R)
        x_t = new("x_t", [DT, T])
        x_fin = at("x_fin", [TB, D], a_at)
        gain_fin = at("gain_fin", [1, D], a_at + size([TB, D]))

        shared = top[0]
        top[0] += 88 * 1024
        KB = 1024
        qf = at("qf", [2 * H, T], shared)
        q_a = qf[:, 0:H]
        f_a = qf[:, H:2 * H]
        g_a = at("g_a", [3, H, T], shared + 16 * KB)
        q_b, k_b = g_a[:, 1], g_a[:, 2]
        val = at("val", [2, TB, DM], shared + 40 * KB)
        gates = at("gates", [2 * DT, T], shared + 56 * KB)
        wide_b = at("wide_b", [LEVELS, T], shared + 64 * KB)
        x_tok = at("x_tok", [TB, D], shared + 56 * KB)
        keys = at("keys", [H, T], shared + 72 * KB)
        masks = at("masks", [MASKED, P], shared + 80 * KB)
        masked = at("masked", [MASKED, P], shared + 80 * KB + size([MASKED, P]))
        ya_hi = at("ya_hi", [H, T], shared + 8 * KB, F32R)
        ya_lo = at("ya_lo", [H, T], shared + 16 * KB, F32R)
        m_hi = at("m_hi", [DT, T], shared, F32R)
        m_lo = at("m_lo", [DT, T], shared + 16 * KB, F32R)
        f_hi = at("f_hi", [T], shared + 80 * KB, F32R)
        f_lo = at("f_lo", [T], shared + 81 * KB, F32R)
        ff_hi = at("ff_hi", [FT, T], shared, F32R)
        ff_lo = at("ff_lo", [FT, T], shared + 44 * KB, F32R)
        v_g = at("v_g", [G, TB, NB], shared)
        y_lo = at("y_lo", [ET, T], shared, F32R)
        y_hi = at("y_hi", [ET, T], shared + 32 * KB, F32R)
        v_one = at("v_one", [TB, NB], shared + 64 * KB)
        u_act = at("u_act", [4, T], shared + 68 * KB)
        g_act = at("g_act", [4, T], shared + 72 * KB)
        y_one = at("y_one", [4, T], shared + 76 * KB)
        ws_t = at("ws_t", [TB, G, P], shared + 80 * KB)

        wide_at = top[0]
        wide = new("wide", [LEVELS, T])
        wide4 = wide[:].rearrange("p a t -> p (a t)")
        ws_raw = at("ws_raw", [G, P], wide_at + 4 * KB)
        bs_all = at("bs_all", [G, P], wide_at)
        scan_at = top[0]
        scan = new("scan", [T])
        part = at("part", [T], scan_at)
        ident = new("ident", [P])
        flip = new("flip", [P])
        ones = new("ones", [P])
        p_t = new("p_t", [3 * P])
        vec_rows = at("vec_rows", [2, P], top[0])
        p_n = new("p_n", [3 * P])
        v_head = new("v_head", [TB, DH])
        q_head = new("q_head", [T])
        rstd = at("rstd", [1, T], top[0])
        hank = new("hank", [T])
        total_at = top[0]
        total = new("total", [T])
        vec = new("vec", [2, P])
        lbw = new("lbw", [8, H])
        ident_r = new("ident_r", [H], F32R)
        small = new("small", [64])
        assert top[0] <= nc.sbuf_usable_end, top[0]
        ext_sb = p_t[0:H, 0:EXT]
        decay = [wide, wide_b]
        key_head = [q_head, hank]
        GAIN_MIX, GAIN_FFN, GAIN_A, B_GATE, V_GAIN, ROWS0 = 0, 16, 32, 48, 80, 112
        LB0, LB1, OUT_GAIN, Q_GAIN, K_GAIN, ROWS1 = 0, 8, 16, 24, 25, 26
        col = lambda c: vec[:, 0, c:c + 1]
        eps_c, gq_c = small[:, 0:1], small[:, 1:2]
        ssx, rx = small[:, 2:4], small[:, 4:6]
        mneg, psum_, rsum = small[:, 6:8], small[:, 8:10], small[:, 10:12]
        rv, rf = small[:, 12:14], small[:, 14:16]
        ssv = small[:, 16:32].rearrange("p (b g) -> p b g", b=TB)
        ssf = small[:, 32:40].rearrange("p (b g) -> p b g", b=TB)
        tot = small[:, 40:42]
        mpos = small[:, 42:44]
        r_tok = small[:, 44:46]
        pick = small[:, 46:46 + 2 * H - 1]
        r_x = at("r_x", [1, T], total_at)

        gp = ctx.enter_context(nc.psum_tensor("gp", [P, 2, 2, NB], F32))
        mx = ctx.enter_context(nc.psum_tensor("mx", [P, 4, NB], F32))

        ext = nc.dram_tensor("ext", [H, EXT], F32, kind="Internal").ap()
        hankel = nc.dram_tensor("hankel", [H, P, T], F32, kind="Internal").ap()

        def sem(name):
            return ctx.enter_context(nc.semaphore(name))

        raw_in = [sem(f"raw_in{s}") for s in range(RING)]
        hi_ready = sem("hi_ready")
        lo_ready = sem("lo_ready")
        unit_used = sem("unit_used")
        bank_free = [sem(f"bank_free{i}") for i in range(2)]
        op_hi = sem("op_hi")
        op_ready = sem("op_ready")
        gated = sem("gated")
        scale_ready = sem("scale_ready")
        x_in = [sem(f"x_in{i}") for i in range(2 * TB)]
        vec_in = sem("vec_in")
        rel_in = sem("rel_in")
        ext_made = sem("ext_made")
        ext_out = sem("ext_out")
        hankel_out = sem("hankel_out")
        consts = sem("consts")
        gp_self = sem("gp_self")
        gain_mix_in = sem("gain_mix_in")
        x_rooted = sem("x_rooted")
        x_inverse = sem("x_inverse")
        x_spread = sem("x_spread")
        gates_ready = sem("gates_ready")
        act_self = sem("act_self")
        dve_self = sem("dve_self")
        turned = sem("turned")
        turned_out = sem("turned_out")
        vec_t = sem("vec_t")
        vec_ready = sem("vec_ready")
        lb_exp = sem("lb_exp")
        lb_max = sem("lb_max")
        sums = sem("sums")
        sums2 = sem("sums2")
        rstd_ready = sem("rstd_ready")
        evac_v = sem("evac_v")
        sig_ready = sem("sig_ready")
        silu_ready = sem("silu_ready")
        pre_ready = sem("pre_ready")
        ln_ready = sem("ln_ready")
        z_ready = sem("z_ready")
        e_ready = sem("e_ready")
        qk_ready = sem("qk_ready")
        prod_done = sem("prod_done")
        p_ready = sem("p_ready")
        cross_copied = sem("cross_copied")
        v_ready = sem("v_ready")
        head_ready = sem("head_ready")
        pv_done = sem("pv_done")
        o_copied = sem("o_copied")
        sq_ready = sem("sq_ready")
        ms_done = sem("ms_done")
        factors_ready = sem("factors_ready")
        factors_spread = sem("factors_spread")
        factors_used = sem("factors_used")
        qk_normed = sem("qk_normed")
        norm_part = sem("norm_part")
        hank_in = sem("hank_in")
        s_done = sem("s_done")
        max_done = sem("max_done")
        exp_done = sem("exp_done")
        pn_ready = sem("pn_ready")
        pt_done = sem("pt_done")
        pt_copied = sem("pt_copied")
        ws_in = sem("ws_in")
        bs_in = sem("bs_in")
        ws_turned = sem("ws_turned")
        ws_ready = sem("ws_ready")
        sv_done = sem("sv_done")
        sv_used = sem("sv_used")
        v_one_in = sem("v_one_in")
        mixer_ready = sem("mixer_ready")
        fin_turned = sem("fin_turned")
        fin_copied = sem("fin_copied")
        gain_in = sem("gain_in")
        fin_squared = sem("fin_squared")
        rows_a = sem("rows_a")
        rows_v = sem("rows_v")
        out_done = sem("out_done")

        a_op, ff_op, y_op = (a_hi, a_lo), (ff_hi, ff_lo), (y_hi, y_lo)
        ya_op, m_op = (ya_hi, ya_lo), (m_hi, m_lo)
        S = [
            Segment(w_in, "T", 2, D, (0, NB), 2 * NB, a_op),
            Segment(w_in, "N", 2, D, (2 * DM, 2 * DM + NB), 4 * DM, a_op),
            Segment(w_in, "T", 3, D, (3 * DM, 3 * DM + NB), 2 * NB, a_op),
            Segment(w_in, "T", 4, D, (7 * DM, 7 * DM + NB), 2 * NB, a_op),
            Segment(w_proj_a, "T", 2, DM, (0, NB), 2 * NB, ya_op),
            Segment(w_proj_b, "T", 2, DM, (0, NB), 2 * NB, a_op),
            Segment(w_out, "T", 2, D, (0, NB), 2 * NB, m_op),
            Segment(w_ffn_in, "T", FF // NB, D, (0, FF), NB, a_op),
            Segment(w_ffn_out, "T", 2, FF, (0, NB), 2 * NB, ff_op),
            Segment(a_w_in, "N", 4, D, (E2, E2 + NB), 2 * NB, a_op),
            Segment(a_w_in, "T", G, D, (0, 2 * E2), NB, a_op),
            Segment(a_w_out, "N", 2, E2, (0, NB), 2 * NB, y_op),
        ]
        QF, IV, GQK, GATES, PROJ_A, PROJ_B, OUT, FFN_IN, FFN_OUT, V_IN, UG_IN, Y_OUT = range(len(S))
        unit0, block0 = [0], [0]
        for s in S:
            unit0.append(unit0[-1] + s.steps * s.pair)
            block0.append(block0[-1] + s.steps * 2)
        OPS = {QF: DT, PROJ_A: H, PROJ_B: H, OUT: DT, FFN_IN: DT, FFN_OUT: FT, V_IN: DT, Y_OUT: ET}
        ALONE = (QF, FFN_IN, FFN_OUT, V_IN, Y_OUT)
        op0, hi0, n, n_hi = {}, {}, 0, 0
        for k in range(len(S)):
            op0[k], hi0[k] = n, n_hi
            n += OPS.get(k, 0)
            n_hi += 0 if k in ALONE else OPS.get(k, 0)

        def after(k, i, units):
            return i * S[k].pair + (unit0[k] + units)

        block = ctx.enter_context(nc.Block())

        @block.sync
        def _(sp):
            def load_x(c):
                half = slice(c * D // 2, (c + 1) * D // 2)
                for b in range(TB):
                    sp.dma_start(x_tok[:, b, half], x[b * P:(b + 1) * P, half]).then_inc(x_in[c * TB + b], 16)

            load_x(0)

            def load(k, i):
                s = S[k]
                for j in range(s.pair):
                    if (k, i, j) == (0, 0, 1):
                        load_x(1)
                    if (k, i) != (0, 0) or j >= RING:
                        sp.wait_ge(lo_ready, after(k, i, j + 1 - RING))
                    u = j % s.units
                    c = s.first[j // s.units]
                    src = s.w[u * UK * P:(u + 1) * UK * P, bass.ds(i * s.stride + c, NB)]
                    sp.dma_start(raw[:, j % RING], src.rearrange("(k p) n -> p k n", p=P)).then_inc(
                        raw_in[j % RING], 16)

            load(0, 0)
            with sp.Fori(1, S[0].steps) as i:
                load(0, i)
            for k in range(1, len(S)):
                with sp.Fori(0, S[k].steps) as i:
                    load(k, i)
            for c in range(2):
                half = slice(c * D // 2, (c + 1) * D // 2)
                for b, rows in ((1, rows_v), (0, rows_a)):
                    sp.wait_ge(rows, c + 1)
                    sp.dma_start(out[b * P:(b + 1) * P, half], x_fin[:, b, half]).then_inc(out_done, 16)
            sp.wait_ge(out_done, 16 * 2 * TB)

        @block.gpsimd
        def _(pool):
            own = Chain(pool, gp_self)
            own.link(pool.memset(ident[:], 0.0))
            own.link(pool.memset(flip[:], 0.0))
            pool.affine_select(out=ident[:], in_=ident[:], compare_op=ALU.not_equal, fill=1.0, base=0,
                               pattern=[[-1, P]], channel_multiplier=1).then_inc(consts, 1)
            pool.affine_select(out=flip[:], in_=flip[:], compare_op=ALU.not_equal, fill=1.0,
                               base=1 - P, pattern=[[1, P]], channel_multiplier=1).then_inc(consts, 1)
            rows = [(0, 16, norm_ffn, 16), (0, 32, a_norm, 16), (0, 48, b_gate, 32),
                    (0, 80, a_v_gain, 32), (1, 0, lb_logits, 16), (1, 16, out_gain, 8), (1, 24, q_gain, 1),
                    (1, 25, k_gain, 1)]
            for which, r, src, n in rows:
                pool.dma_start(vec_rows[r:r + n, which], src.rearrange("(r n) -> r n", n=P)).then_inc(vec_in, 16)
            pool.dma_start(p_t[0:H, REL_FUTURE + 1:REL_FUTURE + 1 + N_REL], rel_bias).then_inc(rel_in, 16)
            own.link(pool.memset(masks[:], 0.0))
            pool.affine_select(out=masks[:, 0], in_=masks[:, 0], compare_op=ALU.not_equal, fill=1.0,
                               base=0, pattern=[[-1, P]], channel_multiplier=1).then_inc(consts, 1)
            for l in range(MASKED - 1):
                w = 1 << l
                half = masks[:, 1 + l].rearrange("p (b h j) -> p b h j", h=2, j=w)[:, :, 1, :]
                own.link(pool.memset(half, 1.0))
                own.link(pool.affine_select(out=half, in_=half, compare_op=ALU.is_ge, fill=0.0, base=0,
                                            pattern=[[-2 * w, P // (2 * w)], [0, w]], channel_multiplier=1))
                pool.affine_select(out=half, in_=half, compare_op=ALU.is_ge, fill=0.0, base=w - 1,
                                   pattern=[[2 * w, P // (2 * w)], [0, w]],
                                   channel_multiplier=-1).then_inc(consts, 1)

            pool.wait_ge(ext_made, 1)
            pool.dma_start(ext, ext_sb).then_inc(ext_out, 16)
            pool.wait_ge(ext_out, 16)
            pool.dma_start(hankel, bass.AP(ext.tensor, 0, [[EXT, H], [1, P], [1, T]])).then_inc(hankel_out, 16)

            def weigh(h, buf):
                pool.wait_ge(e_ready, h + 1)
                pool.tensor_copy(key_head[buf][:], keys[:, bass.ds(h, 1)].rearrange("p a t -> p (a t)")).then_inc(head_ready, 1)
                for l in range(LEVELS):
                    w = 1 << l
                    two = decay[buf][:, l].rearrange("p (b h j) -> p b h j", h=2, j=w)
                    qh = q_a[:, bass.ds(h, 1)].rearrange("p a (b h j) -> p (a b) h j", h=2, j=w)
                    kh = keys[:, bass.ds(h, 1)].rearrange("p a (b h j) -> p (a b) h j", h=2, j=w)
                    pool.tensor_tensor(two[:, :, 1, :], two[:, :, 1, :], qh[:, :, 1, :], ALU.mult)
                    last = pool.tensor_tensor(two[:, :, 0, :], two[:, :, 0, :], kh[:, :, 0, :], ALU.mult)
                last.then_inc(qk_ready, 1)

            def head_values(h, which):
                pool.wait_ge(pv_done, h + (H * which + 1))
                pool.tensor_copy(v_head[:], val[:, which, :, bass.ds(h * DH, DH)]).then_inc(v_ready, 1)

            pool.wait_ge(pre_ready, 2)
            weigh(0, 0)
            pool.wait_ge(bank_free[1], 1 + block0[IV] // 2 + 1)
            head_values(0, 0)
            with pool.Fori(0, H // 2 - 1) as i:
                weigh(i * 2 + 1, 1)
                head_values(i * 2 + 1, 0)
                weigh(i * 2 + 2, 0)
                head_values(i * 2 + 2, 0)
            weigh(H - 1, 1)
            head_values(H - 1, 0)
            pool.wait_ge(sig_ready, 3)
            pool.tensor_tensor(keys[:], keys[:], g_a[:, 0], ALU.mult).then_inc(silu_ready, 1)
            pool.wait_ge(prod_done, 3 * H + 1)
            pool.wait_ge(hankel_out, 16)
            with pool.Fori(0, H) as h:
                pool.wait_ge(s_done, h + 1)
                pool.dma_start(hank[:], hankel[bass.ds(h, 1)].rearrange("a p t -> p (a t)")).then_inc(hank_in, 16)
                pool.wait_ge(qk_normed, 1)
                pool.tensor_copy(q_head[:], g_a[:, 1, bass.ds(h, 1)].rearrange("p a t -> p (a t)")).then_inc(head_ready, 1)
                head_values(h, 1)
            pool.wait_ge(op_ready, op0[V_IN] + DT)
            pool.dma_start(ws_raw[:], a_w_s.rearrange("g p q -> p g q")).then_inc(ws_in, 16)
            pool.wait_ge(sums, 1)
            pool.dma_start(bs_all[:].rearrange("p g n -> p (g n)"), a_b_s.partition_broadcast(P)).then_inc(bs_in, 16)
            with pool.Fori(0, G) as g:
                pool.wait_ge(sv_done, g + 1)
                pool.tensor_copy(v_one[:], v_g[:, bass.ds(g, 1)].rearrange("p a b n -> p (a b) n")).then_inc(v_one_in, 1)
            pool.wait_ge(unit_used, unit0[Y_OUT])
            pool.dma_start(gain_fin[:, 0], final_norm.partition_broadcast(P)).then_inc(gain_in, 16)

        @block.scalar
        def _(act):
            own = Chain(act, act_self)

            def split(slot, use, used):
                act.wait_ge(raw_in[slot], use)
                if used is not None:
                    act.wait_ge(unit_used, used)
                act.activation(w_hi[:, slot], raw[:, slot], ACT.Copy).then_inc(hi_ready, 1)

            def step(k, i, evac, last=False, mid=None):
                s = S[k]
                for j in range(s.pair):
                    if not (last and j >= s.pair - RING):
                        n = unit0[k] + RING + j
                        split(j % RING, i * (16 * s.pair // RING) + 16 * (n // RING + 1),
                              after(k, i, j + 1))
                    if j % s.units == s.units - 1:
                        b = j // s.units
                        act.wait_ge(unit_used, after(k, i, j + 1))
                        evac(i, b)
                    if mid is not None:
                        mid(i, j)

            def run(k, evac, per=0, final=False, mid=None, begin=0, end=None):
                steps = (S[k].steps if end is None else end) - final
                if steps - begin == 1:
                    step(k, begin, evac, mid=mid)
                else:
                    with act.Fori(begin, steps) as i:
                        own.enter(i - begin if begin else i, per)
                        step(k, i, evac, mid=mid)
                        own.leave(steps - begin)
                if final:
                    step(k, steps, evac, last=True, mid=mid)

            def none(i, b):
                pass

            act.dma_start(vec_rows[0:DT, 0], norm_mix.rearrange("(r n) -> r n", n=P)).then_inc(gain_mix_in, 16)
            act.wait_ge(vec_ready, 1)
            for g in range(8):
                act.wait_ge(turned, g + 1)
                for m in (2 * g, 2 * g + 1):
                    act.activation(a_hi[:, m], mx[:, g % 4, (m % 2) * T:(m % 2 + 1) * T], ACT.Copy, scale=col(GAIN_MIX + m))
                act.activation(x_t[:, 2 * g:2 * g + 2].rearrange("p m t -> p (m t)"), mx[:, g % 4], ACT.Copy).then_inc(
                    turned_out, 1)
                if g < RING:
                    split(g, 16, None)
            for c in range(2):
                act.wait_ge(x_in[c * TB], 16)
            own.link(act.activation(wide4, x_tok[:, 0], ACT.Square, accum_out=ssx[:, 0:1]))
            act.wait_ge(lb_max, 1)
            act.activation(lbw[:, 2:4], lbw[:, 2:4], ACT.Exp).then_inc(lb_exp, 1)

            act.sem_inc(o_copied, 1)
            act.sem_inc(exp_done, 1)

            def rms(dst, src, dim):
                return act.activation(dst, src, ACT.Sqrt, scale=1.0 / dim, bias=eps_c[0:dst.shape[0]])

            def x_root(i, j):
                if j == 1:
                    own.link(act.activation(wide4, x_tok[:, 1], ACT.Square, accum_out=ssx[:, 1:2]))
                if j == 3:
                    rms(rx, ssx, D).then_inc(x_rooted, 1)

            run(QF, none, mid=x_root, end=1)
            run(QF, none, begin=1)
            act.wait_ge(x_inverse, 1)

            def copied(k):
                for b in range(2):
                    act.wait_ge(bank_free[b], 1 + block0[k + 1] // 2)

            def decay_exp(h, buf):
                act.wait_ge(z_ready, h + 1)
                act.activation(decay[buf][:], decay[buf][:], ACT.Exp).then_inc(e_ready, 1)

            def hgrn_first(i, j):
                if j == 0:
                    copied(QF)
                    act.activation(wide[:], q_a, ACT.Sigmoid).then_inc(sig_ready, 1)
                if j == 1:
                    act.activation(f_a, f_a, ACT.Sigmoid).then_inc(sig_ready, 1)
                if j == 4:
                    act.wait_ge(pre_ready, 1)
                    act.activation(f_a, f_a, ACT.Ln).then_inc(ln_ready, 1)
                if j == 11:
                    decay_exp(0, 0)

            def val_out(i, b):
                for t in range(TB):
                    ins = act.activation(val[:, bass.ds(i, 1), t, b * NB:(b + 1) * NB].rearrange("p a n -> p (a n)"), gp[:, b, t],
                                         ACT.Copy, scale=rx[:, t:t + 1])
                ins.then_inc(bank_free[b], 1)

            run(IV, val_out, mid=hgrn_first, end=1)
            run(IV, val_out, begin=1)

            def cross_copy(h):
                act.wait_ge(prod_done, h * 3 + 4)
                act.wait_ge(pv_done, h + 1)
                act.activation(p_t[:, P:2 * P], mx[:, 3, 0:P], ACT.Copy).then_inc(cross_copied, 1)

            def hgrn(i, j):
                h, u, b = i * 2 + j // 8, j % 8, j // 8
                if u == 2 and not (isinstance(i, int) and b == 1):
                    decay_exp(h + 1, 1 - b)
                if u == 5:
                    cross_copy(h)
                if u == 7:
                    act.wait_ge(pv_done, h + 2)
                    act.activation(q_a[:, bass.ds(h, 1)].rearrange("p a t -> p (a t)"), mx[:, 3, T:2 * T], ACT.Copy).then_inc(o_copied, 1)

            run(GQK, none, mid=hgrn)

            def gate_sigmoid(i, tile0):
                for m in range(4):
                    one = gates[:, bass.ds(tile0 + m, 1)]
                    ins = act.activation(one, one, ACT.Sigmoid, bias=vec[:, 0, bass.ds(tile0 + (B_GATE + m), 1)])
                ins.then_inc(gates_ready, 1)

            def gates_before(i, half):
                act.wait_ge(bank_free[half], i + (block0[GATES] // 2 + 1))
                gate_sigmoid(i, i * 8 + (4 * half - 8))

            def squares(r):
                if r:
                    act.wait_ge(ms_done, r)
                act.activation(wide[:], (q_a, q_b, k_b)[r], ACT.Square).then_inc(sq_ready, 1)

            def hgrn_end(i, j):
                hgrn(i + 3, j)
                if j == 15:
                    copied(GQK)
                    act.wait_ge(o_copied, H + 1)
                    squares(0)

            def norms(i, j):
                if j in (3, 7):
                    squares(j // 4 + 1)
                for r in range(3):
                    if j == 4 * r + 1:
                        act.wait_ge(ms_done, r + 1)
                        rms(part[0:H], mx[0:H, 2, 0:T], DH).then_inc(rstd_ready, 1)
                if j == 0:
                    act.activation(keys[:], g_a[:, 0], ACT.Sigmoid).then_inc(sig_ready, 1)
                if j in (0, 13):
                    gates_before(i, j // 13)
                if j == 8:
                    act.wait_ge(mixer_ready, 1)
                    act.activation(ya_hi[:], q_a, ACT.Copy).then_inc(op_hi, H)

            def attention(i, j):
                h, u = (i - 2) * 4 + j // 4, j % 4
                if u == 0:
                    act.wait_ge(max_done, h + 1)
                    act.activation(p_n[:, 0:P], mx[:, 0, 0:P], ACT.Exp, bias=mneg[:, 0:1], accum_out=psum_[:, 0:1])
                    act.activation(p_n[:, P:3 * P], mx[:, 0, P:3 * P], ACT.Exp, bias=mneg[:, 1:2],
                                   accum_out=psum_[:, 1:2]).then_inc(exp_done, 1)
                if j in (1, 9):
                    gates_before(i, j // 8)
                if u == 2:
                    act.wait_ge(pt_done, h + 1)
                    act.activation(p_t[:], mx[:, 1, 0:3 * P], ACT.Copy).then_inc(pt_copied, 1)
                if u == 3:
                    act.wait_ge(pv_done, h + (H + 2))
                    act.activation(g_a[:, 1, bass.ds(h, 1)].rearrange("p a t -> p (a t)"), mx[:, 3, T:2 * T], ACT.Copy).then_inc(o_copied, 1)

            run(GATES, none, mid=hgrn_end, end=1)
            run(GATES, none, mid=norms, begin=1, end=2)
            run(GATES, none, mid=attention, begin=2)
            act.wait_ge(unit_used, unit0[PROJ_A])
            act.wait_ge(o_copied, 2 * H + 1)
            for c in range(2):
                act.activation(a_hi[:, 4 * c:4 * c + 4], q_b[:, 4 * c:4 * c + 4], ACT.Copy).then_inc(op_hi, 4)

            def last_gates(i, j):
                if j == 2:
                    for b in range(2):
                        act.wait_ge(bank_free[b], block0[GATES] // 2 + 1 + S[GATES].steps)
                    gate_sigmoid(i, i * 4 + (2 * DT - 8))

            run(PROJ_A, none, mid=last_gates)

            def merged(i, b):
                act.wait_ge(evac_v, i * 2 + (b + 1))
                act.activation(m_hi[:, bass.ds(i * 8 + 4 * b, 4)], gates[:, bass.ds(i * 8 + 4 * b, 4)], ACT.Copy).then_inc(op_hi, 4)

            run(PROJ_B, merged)

            def residual(r):
                def evac(i, b):
                    act.wait_ge(evac_v, i * 2 + (5 + 4 * r + b))
                    act.activation(wide[:, 0:4], x_t[:, bass.ds(i * 8 + 4 * b, 4)], ACT.Square).then_inc(sq_ready, 1)
                return evac

            def norm_root(i, j):
                if j == 4:
                    act.wait_ge(ms_done, 4)
                    rms(rstd[:, 0], mx[:, 2, 0:T], D).then_inc(rstd_ready, 1)

            run(OUT, residual(0))

            def ffn(i, b):
                if b == 0:
                    act.wait_ge(bank_free[0], i + (block0[FFN_IN] // 2 + 2))
                    act.activation(wide[:, 0:4], wide[:, 0:4], ACT.Silu).then_inc(gated, 1)

            run(FFN_IN, ffn, mid=norm_root, end=1)
            run(FFN_IN, ffn, begin=1)
            run(FFN_OUT, residual(1))

            def v_first(i, j):
                if j == 4:
                    act.wait_ge(ms_done, 6)
                    rms(rstd[:, 0], mx[:, 2, 0:T], D).then_inc(rstd_ready, 1)
                    rms(r_tok, mx[:, 3, 0:TB], D).then_inc(rstd_ready, 1)
                if j == 6:
                    act.wait_ge(scale_ready, 1)

            def v_out(i, b):
                for t in range(TB):
                    dst = v_g[:, bass.ds(i * 2 + b, 1), t].rearrange("p a n -> p (a n)")
                    own.link(act.activation(dst, gp[:, b, t], ACT.Gelu_apprx_tanh, scale=r_tok[:, t:t + 1]))
                for t in range(TB):
                    dst = v_g[:, bass.ds(i * 2 + b, 1), t].rearrange("p a n -> p (a n)")
                    ins = act.activation(wide4[:, t * NB:(t + 1) * NB], dst, ACT.Square,
                                         accum_out=ssv[:, t, bass.ds(i * 2 + b, 1)])
                own.link(ins)
                act.sem_inc(bank_free[b], 1)

            run(V_IN, v_out, mid=v_first, end=1)
            run(V_IN, v_out, per=6, begin=1)
            act.sem_inc(sums, 1)
            act.wait_ge(sums2, 1)
            rms(rv, tot, E2).then_inc(rstd_ready, 1)

            def ug(i, b):
                if b == 0:
                    act.wait_ge(bank_free[0], i + (block0[UG_IN] // 2 + 2))
                    act.activation(u_act[:], u_act[:], ACT.Gelu_apprx_tanh).then_inc(gated, 1)
                else:
                    act.wait_ge(bank_free[1], i + (block0[UG_IN] // 2 + 2))
                    act.activation(g_act[:], g_act[:], ACT.Silu).then_inc(gated, 1)

            run(UG_IN, ug)

            def x_turned(i, j):
                g = j - 1
                if i == 0 and 0 <= g < 8:
                    act.wait_ge(fin_turned, g + 1)
                    b, c = g // 4, g % 4
                    act.activation(x_fin[:, b, c * NB:(c + 1) * NB], mx[:, g % 4], ACT.Copy).then_inc(fin_copied, 1)
                if (i, j) == (1, 20):
                    act.activation(mpos[:, 0:1], eps_c, ACT.Sqrt)

            def fin(i, b):
                for t in range(TB):
                    act.wait_ge(evac_v, 13 + 2 * (2 * i + b) + t)
                    ins = act.activation(wide4[:, t * NB:(t + 1) * NB], x_fin[:, t, (2 * i + b) * NB:(2 * i + b + 1) * NB],
                                         ACT.Square, accum_out=ssf[:, t, 2 * i + b:2 * i + b + 1])
                own.link(ins)
                act.sem_inc(fin_squared, 1)

            run(Y_OUT, fin, final=True, mid=x_turned)
            act.wait_ge(sums2, 2)
            rms(rf, tot, D).then_inc(rstd_ready, 1)
            act.wait_ge(scale_ready, 2)
            for c in range(2):
                half = x_fin[:, 0, c * D // 2:(c + 1) * D // 2]
                act.activation(half, half, ACT.Copy, scale=rf[:, 0:1]).then_inc(rows_a, 1)

        @block.vector
        def _(dve):
            own = Chain(dve, dve_self)

            def split(slot, n):
                dve.wait_ge(hi_ready, n)
                dve.tensor_tensor(w_lo[:, slot], raw[:, slot], w_hi[:, slot], ALU.subtract).then_inc(lo_ready, 1)

            def step(k, i, evac, last=False, mid=None):
                s = S[k]
                for j in range(s.pair):
                    if not (last and j >= s.pair - RING):
                        split(j % RING, after(k, i, RING + j + 1))
                    if j % s.units == s.units - 1:
                        b = j // s.units
                        dve.wait_ge(unit_used, after(k, i, j + 1))
                        evac(i, b)
                    if mid is not None:
                        mid(i, j)

            def run(k, evac, per=0, final=False, mid=None, begin=0, end=None):
                steps = (S[k].steps if end is None else end) - final
                if steps - begin == 1:
                    step(k, begin, evac, mid=mid)
                else:
                    with dve.Fori(begin, steps) as i:
                        own.enter(i - begin if begin else i, per)
                        step(k, i, evac, mid=mid)
                        own.leave(steps - begin)
                if final:
                    step(k, steps, evac, last=True, mid=mid)

            def none(i, b):
                pass

            dve.memset(small[:, 0:1], EPS)
            dve.memset(gp[:, 0, 0, 0:1], 0.0).then_inc(bank_free[0], 1)
            dve.memset(gp[:, 1, 0, 0:1], 0.0).then_inc(bank_free[1], 1)
            dve.memset(ones[:], 1.0)
            own.link(dve.memset(pick, 0.0))
            dve.memset(pick[:, H - 1:H], 1.0)
            dve.wait_ge(vec_t, 1)
            dve.tensor_copy(vec[:, 0, 0:DT], gp[:, 1, 0, 0:DT]).then_inc(vec_ready, 1)
            dve.wait_ge(vec_ready, 1)
            for g in range(8):
                dve.wait_ge(turned_out, g + 1)
                for m in (2 * g, 2 * g + 1):
                    ins = dve.scalar_tensor_tensor(out=a_lo[:, m], in0=x_t[:, m], scalar=col(GAIN_MIX + m),
                                                   in1=a_hi[:, m].bitcast(F32), op0=ALU.mult, op1=ALU.subtract)
                ins.then_inc(op_ready, 2)
                if g < RING:
                    split(g, g + 1)
            dve.wait_ge(rel_in, 16)
            dve.tensor_copy(ext_sb[:, 0:REL_FUTURE + 1], ext_sb[:, REL_FUTURE + 1:REL_FUTURE + 2].broadcast_to([H, REL_FUTURE + 1]))
            e = REL_FUTURE + 1 + N_REL
            dve.tensor_copy(ext_sb[:, e:EXT], ext_sb[:, e - 1:e].broadcast_to([H, EXT - e])).then_inc(ext_made, 1)
            dve.wait_ge(vec_t, 2)
            dve.tensor_copy(vec[:, 0, DT:ROWS0], gp[:, 1, 0, DT:ROWS0])
            own.link(dve.tensor_copy(vec[:, 1, 0:ROWS1], gp[:, 1, 1, 0:ROWS1]))
            own.link(dve.tensor_scalar(gq_c, vec[:, 1, Q_GAIN:Q_GAIN + 1], DH ** -0.5, None, ALU.mult))
            dve.sem_inc(vec_ready, 1)
            own.link(dve.tensor_copy(ident_r[:], ident[:, 0:H]))
            l0, l1 = vec[:, 1, LB0:LB0 + H], vec[:, 1, LB1:LB1 + H]
            own.link(dve.tensor_tensor(lbw[:, 0], l0, l1, ALU.max))
            dve.tensor_tensor(lbw[:, 2], l0, lbw[:, 0], ALU.subtract)
            dve.tensor_tensor(lbw[:, 3], l1, lbw[:, 0], ALU.subtract).then_inc(lb_max, 1)
            dve.wait_ge(lb_exp, 1)
            own.link(dve.tensor_tensor(lbw[:, 0], lbw[:, 2], lbw[:, 3], ALU.add))
            own.link(dve.reciprocal(lbw[:, 1], lbw[:, 0]))
            own.link(dve.tensor_tensor(lbw[:, 4], lbw[:, 2], lbw[:, 1], ALU.mult))
            own.link(dve.tensor_scalar(lbw[:, 5], lbw[:, 4], -1.0, 1.0, ALU.mult, ALU.add))

            dve.sem_inc(p_ready, 1)
            dve.sem_inc(sv_used, 1)

            def scaled(dst, b, factors=rstd):
                dve.tensor_tensor(dst, gp[:, b].rearrange("p a (c t) -> p (a c) t", c=2), factors[:].broadcast_to([P, 4, T]),
                                  ALU.mult).then_inc(bank_free[b], 1)

            def invert_x(i, j):
                if j == 4:
                    dve.wait_ge(x_rooted, 1)
                    own.link(dve.reciprocal(rx, rx))
                    own.link(dve.tensor_scalar(mpos, ssx, 1.0 / D, EPS, ALU.mult, ALU.add))
                    own.link(dve.tensor_tensor(mneg, rx, rx, ALU.mult))
                    own.link(dve.tensor_tensor(mneg, mneg, mpos, ALU.mult))
                    own.link(dve.tensor_scalar(mneg, mneg, -0.5, 1.5, ALU.mult, ALU.add))
                    own.link(dve.tensor_tensor(rx, rx, mneg, ALU.mult))
                    for b in range(TB):
                        ins = dve.tensor_scalar(scan[:, b * P:(b + 1) * P], ident[:], rx[:, b:b + 1], None, ALU.mult)
                    ins.then_inc(x_inverse, 1)
                if j == 6:
                    dve.wait_ge(x_spread, 1)
                    own.link(dve.tensor_copy(r_x[:, 0], mx[:, 2, 0:T]))

            def qf_out(i, b):
                scaled(qf[:, bass.ds(i * 8 + 4 * b, 4)], b, r_x)

            run(QF, qf_out, mid=invert_x, end=1)
            run(QF, qf_out, begin=1)

            def decays(h, buf, part_):
                out_ = decay[buf]
                if part_ == 0:
                    sums_within(h)
                for l in range(4 * part_, 4 * part_ + 4 - part_):
                    w = 1 << l
                    b4 = scan[:].rearrange("p (b h j) -> p b h j", h=2, j=w)
                    z4 = out_[:, l].rearrange("p (b h j) -> p b h j", h=2, j=w)
                    ref = b4[:, :, 0, w - 1:w].broadcast_to([P, T // (2 * w), w])
                    if w < CHUNK:
                        dve.tensor_tensor(z4[:, :, 1, :], b4[:, :, 1, :], ref, ALU.subtract)
                    else:
                        dve.tensor_copy(z4[:, :, 1, :], b4[:, :, 1, :])
                    dve.tensor_tensor(z4[:, :, 0, :], ref, b4[:, :, 0, :], ALU.subtract)
                if part_ == 1:
                    z, c1, c2, c3 = out_[:, LEVELS - 1], CHUNK, 2 * CHUNK, 3 * CHUNK
                    dve.tensor_scalar(z[:, c1:c2], scan[:, c1:c2], scan[:, c2 - 1:c2], -1.0, ALU.subtract, ALU.mult)
                    dve.tensor_copy(z[:, c2:c3], scan[:, c2:c3])
                    dve.tensor_scalar(z[:, c3:T], scan[:, c3:T], scan[:, c3 - 1:c3], None, ALU.add)
                    own.link(dve.tensor_scalar(z[:, 0:c1], scan[:, 0:c1], scan[:, c1 - 1:c1], -1.0, ALU.subtract, ALU.mult))
                    dve.tensor_scalar(z[:, 0:c1], z[:, 0:c1], scan[:, c2 - 1:c2], None, ALU.add).then_inc(z_ready, 1)

            def sums_within(h):
                lf = f_a[:, bass.ds(h, 1)].rearrange("p a t -> p (a t)")
                for c in range(T // CHUNK):
                    c0, c1 = c * CHUNK, (c + 1) * CHUNK
                    ins = dve.tensor_tensor_scan(scan[:, c0:c1], ones[:, 0:CHUNK], lf[:, c0:c1], 0.0, ALU.mult, ALU.add)
                own.link(ins)

            def scores(h, b):
                dve.wait_ge(prod_done, h * 3 + (b + 2))
                dve.wait_ge(pv_done, h + 1)
                part8 = mx[:, 0:2].rearrange("p a n -> p (a n)")
                own.link(dve.tensor_tensor(masked[:].rearrange("p l t -> p (l t)"), part8[:, 0:MASKED * P],
                                           masks[:].rearrange("p l t -> p (l t)"), ALU.mult))
                dst = p_t[:, 2 * b * P:(2 * b + 1) * P]
                own.link(dve.tensor_reduce(dst, masked[:].rearrange("p l t -> p t l"), AX_X, ALU.add))
                dve.tensor_tensor(dst[0:CHUNK, CHUNK:P], dst[0:CHUNK, CHUNK:P],
                                  part8[0:CHUNK, MASKED * P:MASKED * P + CHUNK], ALU.add).then_inc(p_ready, 1)

            def hgrn_first(i, j):
                if j == 1:
                    dve.wait_ge(sig_ready, 2)
                    for h in range(H):
                        ins = dve.tensor_scalar(f_a[:, h], f_a[:, h], lbw[:, 5, h:h + 1], lbw[:, 4, h:h + 1], ALU.mult, ALU.add)
                    own.link(ins)
                if j == 2:
                    own.link(dve.tensor_scalar(keys[:], f_a, -1.0, 1.0, ALU.mult, ALU.add))
                if j == 3:
                    dve.tensor_scalar(f_a, f_a, LN_MIN, None, ALU.max).then_inc(pre_ready, 1)
                if j == 5:
                    dve.tensor_tensor(q_a, q_a, wide[:], ALU.mult).then_inc(pre_ready, 1)
                    dve.wait_ge(consts, 2 + MASKED)
                    dve.wait_ge(ln_ready, 1)
                    dve.wait_ge(pre_ready, 2)
                if j in (7, 8):
                    decays(0, 0, j - 7)

            run(IV, none, mid=hgrn_first, end=1)
            run(IV, none, begin=1)

            def hgrn(i, j):
                h, u, b = i * 2 + j // 8, j % 8, j // 8
                if u in (0, 1) and not (isinstance(i, int) and b == 1):
                    if u == 0:
                        dve.wait_ge(prod_done, h * 3 + 1)
                    decays(h + 1, 1 - b, u)
                if u in (2, 5):
                    scores(h, u // 5)

            def gqk_out(i, b):
                scaled(g_a[:, bass.ds(i, 1), 4 * b:4 * b + 4].rearrange("p a c t -> p (a c) t"), b, r_x)

            run(GQK, gqk_out, per=12, mid=hgrn)

            def hgrn_end(i, j):
                hgrn(i + 3, j)

            def norms(i, j):
                flat = lambda a: a.rearrange("p h t -> p (h t)")
                for r, src in enumerate((q_a, q_b, k_b)):
                    if j == 4 * r + 1:
                        dve.wait_ge(rstd_ready, r + 1)
                        own.link(dve.reciprocal(part[0:H], part[0:H]))
                        own.link(dve.tensor_copy(f_hi[0:H], part[0:H]))
                        dve.tensor_tensor(f_lo[0:H], part[0:H], f_hi[0:H].bitcast(F32), ALU.subtract).then_inc(factors_ready, 1)
                    if j == 4 * r + 3:
                        dve.wait_ge(factors_spread, r + 1)
                        factors = mx[:].rearrange("p a (c t) -> p (a c) t", c=2)
                        if r == 0:
                            for h in range(H):
                                ins = dve.scalar_tensor_tensor(out=src[:, h], in0=src[:, h], scalar=vec[:, 1, OUT_GAIN + h:OUT_GAIN + h + 1],
                                                               in1=factors[:, h], op0=ALU.mult, op1=ALU.mult)
                        else:
                            gain = gq_c if r == 1 else vec[:, 1, K_GAIN:K_GAIN + 1]
                            ins = dve.scalar_tensor_tensor(out=flat(src), in0=flat(src), scalar=gain,
                                                           in1=mx[:].rearrange("p a n -> p (a n)"), op0=ALU.mult, op1=ALU.mult)
                        ins.then_inc(factors_used if r < 2 else qk_normed, 1)
                if j == 6:
                    dve.wait_ge(silu_ready, 1)
                    dve.wait_ge(factors_used, 1)
                    dve.tensor_tensor(q_a, q_a, keys[:], ALU.mult).then_inc(mixer_ready, 1)
                if j == 13:
                    dve.wait_ge(op_hi, hi0[PROJ_A] + H)
                    dve.tensor_tensor(ya_lo[:], q_a, ya_hi[:].bitcast(F32), ALU.subtract).then_inc(op_ready, H)

            def attention(i, j):
                h, u = (i - 2) * 4 + j // 4, j % 4
                if u == 0:
                    dve.wait_ge(s_done, h + 2)
                    s3 = mx[:, 0, 0:3 * P]
                    hidden = mx[0:CHUNK, 0, 0:3 * P].rearrange("p (a n) -> p a n", n=P)[:, 0:3:2, CHUNK:P]
                    own.link(dve.memset(hidden, NEG))
                    dve.tensor_reduce(mpos[:, 0:1], s3[:, 0:P], AX_X, ALU.max)
                    own.link(dve.tensor_reduce(mpos[:, 1:2], s3[:, P:3 * P], AX_X, ALU.max))
                    dve.tensor_scalar(mneg, mpos, -1.0, None, ALU.mult).then_inc(max_done, 1)
                if u == 1:
                    dve.wait_ge(exp_done, h + 2)
                    own.link(dve.reciprocal(rsum, psum_))
                    dve.tensor_scalar(p_n[:, 0:P], p_n[:, 0:P], rsum[:, 0:1], None, ALU.mult)
                    dve.tensor_scalar(p_n[:, P:3 * P], p_n[:, P:3 * P], rsum[:, 1:2], None, ALU.mult).then_inc(pn_ready, 1)

            def gate_out(i, b):
                scaled(gates[:, bass.ds(i * 8 + 4 * b, 4)], b, r_x)

            run(GATES, gate_out, mid=hgrn_end, end=1)
            run(GATES, gate_out, mid=norms, begin=1, end=2)
            run(GATES, gate_out, per=12, mid=attention, begin=2)
            for c in range(2):
                dve.wait_ge(op_hi, hi0[PROJ_B] + 4 * c + 4)
                dve.tensor_tensor(a_lo[:, 4 * c:4 * c + 4], q_b[:, 4 * c:4 * c + 4], a_hi[:, 4 * c:4 * c + 4].bitcast(F32),
                                  ALU.subtract).then_inc(op_ready, 4)

            def proj_a(i, b):
                g4 = gates[:, bass.ds(i * 8 + 4 * b, 4)].rearrange("p (a c) t -> p a (c t)", a=2)
                dve.tensor_tensor(g4, gp[:, b], g4, ALU.mult).then_inc(bank_free[b], 1)

            def proj_b(i, b):
                ga = gates[:, bass.ds(i * 8 + 4 * b, 4)].rearrange("p (a c) t -> p a (c t)", a=2)
                gb = gates[:, bass.ds(i * 8 + (DT + 4 * b), 4)].rearrange("p (a c) t -> p a (c t)", a=2)
                own.link(dve.tensor_tensor(gb, gp[:, b], gb, ALU.mult))
                dve.sem_inc(bank_free[b], 1)
                own.link(dve.tensor_tensor(ga, ga, gb, ALU.add))
                dve.sem_inc(evac_v, 1)
                dve.wait_ge(op_hi, i * 8 + (hi0[OUT] + 4 * b + 4))
                four = bass.ds(i * 8 + 4 * b, 4)
                dve.tensor_tensor(m_lo[:, four], gates[:, four], m_hi[:, four].bitcast(F32), ALU.subtract).then_inc(op_ready, 4)

            dve.wait_ge(gates_ready, 2 * S[GATES].steps - 2)
            run(PROJ_A, proj_a)
            dve.wait_ge(gates_ready, 2 * S[GATES].steps)
            run(PROJ_B, proj_b, per=4)

            def residual(r, gain):
                def evac(i, b):
                    x4 = x_t[:, bass.ds(i * 8 + 4 * b, 4)].rearrange("p (a c) t -> p a (c t)", a=2)
                    own.link(dve.tensor_tensor(x4, gp[:, b], x4, ALU.add))
                    dve.sem_inc(evac_v, 1)
                    dve.sem_inc(bank_free[b], 1)
                    for m in range(4):
                        one = bass.ds(i * 8 + (4 * b + m), 1)
                        ins = dve.tensor_scalar(a_hi[:, one], x_t[:, one], vec[:, 0, bass.ds(i * 8 + (gain + 4 * b + m), 1)],
                                                None, ALU.mult)
                    own.link(ins)
                    for m in range(4):
                        one = bass.ds(i * 8 + (4 * b + m), 1)
                        ins = dve.scalar_tensor_tensor(out=a_lo[:, one], in0=x_t[:, one],
                                                       scalar=vec[:, 0, bass.ds(i * 8 + (gain + 4 * b + m), 1)],
                                                       in1=a_hi[:, one].bitcast(F32), op0=ALU.mult, op1=ALU.subtract)
                    ins.then_inc(op_ready, 4)
                    dve.wait_ge(sq_ready, i * 2 + (4 + 4 * r + b))
                    own.link(dve.tensor_reduce(part[:], wide[:, 0:4].rearrange("p m t -> p t m"), AX_X, ALU.add))
                    own.link(dve.tensor_tensor(total[:], total[:], part[:], ALU.add))
                return evac

            own.link(dve.memset(total[:], 0.0))
            run(OUT, residual(0, GAIN_FFN), per=8)
            dve.sem_inc(norm_part, 1)

            def norm_inverse(i, j):
                if j == 5:
                    dve.wait_ge(rstd_ready, 4)
                    own.link(dve.reciprocal(rstd[:], rstd[:]))

            def ffn(i, b):
                if b == 0:
                    scaled(wide[:, 0:4], 0)
                    return
                scaled(wide[:, 4:8], 1)
                dve.wait_ge(bank_free[1], i + (block0[FFN_IN] // 2 + 2))
                dve.wait_ge(gated, i + 1)
                own.link(dve.tensor_tensor(wide[:, 4:8], wide[:, 4:8], wide[:, 0:4], ALU.mult))
                own.link(dve.tensor_copy(ff_hi[:, bass.ds(i * 4, 4)], wide[:, 4:8]))
                dve.tensor_tensor(ff_lo[:, bass.ds(i * 4, 4)], wide[:, 4:8], ff_hi[:, bass.ds(i * 4, 4)].bitcast(F32),
                                  ALU.subtract).then_inc(op_ready, 4)

            run(FFN_IN, ffn, mid=norm_inverse, end=1)
            run(FFN_IN, ffn, per=2, begin=1)
            own.link(dve.memset(total[:], 0.0))
            run(FFN_OUT, residual(1, GAIN_A), per=8)
            dve.sem_inc(norm_part, 1)

            def v_first(i, j):
                if j == 5:
                    dve.wait_ge(rstd_ready, 6)
                    own.link(dve.reciprocal(rstd[:], rstd[:]))
                    dve.reciprocal(r_tok, r_tok).then_inc(scale_ready, 1)

            run(V_IN, none, mid=v_first, end=1)
            run(V_IN, none, begin=1)
            dve.wait_ge(sums, 1)
            own.link(dve.tensor_reduce(tot, ssv, AX_X, ALU.add))
            dve.sem_inc(sums2, 1)
            dve.wait_ge(rstd_ready, 7)
            own.link(dve.reciprocal(rv, rv))
            dve.wait_ge(ws_turned, 1)
            dve.wait_ge(bs_in, 16)
            for t in range(TB):
                ins = dve.tensor_scalar(ws_t[:, t].rearrange("p g n -> p (g n)"),
                                        mx[:, 0:2].rearrange("p a n -> p (a n)"), rv[:, t:t + 1], None, ALU.mult)
            ins.then_inc(ws_ready, 1)

            def ug(i, b):
                if b == 0:
                    scaled(u_act[:], 0)
                    dve.wait_ge(sv_done, i + 2)
                    for c in range(4):
                        ins = dve.scalar_tensor_tensor(
                            out=y_one[:, c].rearrange("p (b t) -> p b t", b=TB),
                            in0=mx[:, c // 2, (c % 2) * T:(c % 2 + 1) * T].rearrange("p (b t) -> p b t", b=TB),
                            scalar=vec[:, 0, bass.ds(i * 4 + (V_GAIN + c), 1)],
                            in1=bs_all[:, bass.ds(i, 1)].broadcast_to([P, TB, P]), op0=ALU.mult, op1=ALU.add)
                    own.link(ins)
                    dve.sem_inc(sv_used, 1)
                    dve.wait_ge(gated, i * 2 + (S[FFN_IN].steps + 1))
                    own.link(dve.tensor_tensor(y_one[:], y_one[:], u_act[:], ALU.mult))
                else:
                    scaled(g_act[:], 1)
                    dve.wait_ge(gated, i * 2 + (S[FFN_IN].steps + 2))
                    own.link(dve.tensor_tensor(y_one[:], y_one[:], g_act[:], ALU.mult))
                    own.link(dve.tensor_copy(y_hi[:, bass.ds(i * 4, 4)], y_one[:]))
                    dve.tensor_tensor(y_lo[:, bass.ds(i * 4, 4)], y_one[:], y_hi[:, bass.ds(i * 4, 4)].bitcast(F32),
                                      ALU.subtract).then_inc(op_ready, 4)

            run(UG_IN, ug, per=4)

            def fin(i, b):
                if (i, b) == (0, 0):
                    dve.wait_ge(fin_copied, 8)
                for t in range(TB):
                    xf = x_fin[:, t, (2 * i + b) * NB:(2 * i + b + 1) * NB]
                    own.link(dve.tensor_tensor(xf, gp[:, b, t], xf, ALU.add))
                    dve.sem_inc(evac_v, 1)
                dve.sem_inc(bank_free[b], 1)

            def times_gain(n):
                dve.wait_ge(fin_squared, n + 1)
                cols = slice(n * NB, (n + 1) * NB)
                return dve.tensor_tensor(x_fin[:, :, cols], x_fin[:, :, cols], gain_fin[:, :, cols].broadcast_to([P, TB, NB]), ALU.mult)

            def fin_gain(i, j):
                if (i, j) == (0, 24):
                    dve.wait_ge(gain_in, 16)
                    times_gain(0)
                if i == 1 and j in (8, 24):
                    times_gain(j // 16 + 1)

            run(Y_OUT, fin, final=True, mid=fin_gain)
            dve.wait_ge(fin_squared, 4)
            own.link(dve.tensor_reduce(tot, ssf, AX_X, ALU.add))
            dve.sem_inc(sums2, 1)
            own.link(times_gain(3))
            dve.wait_ge(rstd_ready, 8)
            own.link(dve.reciprocal(rf, rf))
            dve.sem_inc(scale_ready, 1)
            for c in range(2):
                half = x_fin[:, 1, c * D // 2:(c + 1) * D // 2]
                dve.tensor_scalar(half, half, rf[:, 1:2], None, ALU.mult).then_inc(rows_v, 1)

        @block.tensor
        def _(pe):
            def unit(k, i, j):
                s = S[k]
                hi, lo = s.operand
                b, u, slot = j // s.units, j % s.units, j % RING
                pe.wait_ge(lo_ready, after(k, i, j + 1))
                for kk in range(UK):
                    t = u * UK + kk
                    first = u == 0 and kk == 0
                    last = u == s.units - 1 and kk == UK - 1
                    for m in range(4 if s.form == "T" else 2):
                        for p, (wp, ap) in enumerate(((w_hi, hi), (w_hi, lo), (w_lo, hi))):
                            if s.form == "T":
                                out_ = gp[:, b, m // 2, (m % 2) * T:(m % 2 + 1) * T]
                                stat, mov = wp[:, slot, kk, m * P:(m + 1) * P], ap[:, t, :]
                                start = first and m % 2 == 0 and p == 0
                            else:
                                out_ = gp[:, b, m, :]
                                stat, mov = ap[:, t, m * P:(m + 1) * P], wp[:, slot, kk, :]
                                start = first and p == 0
                            ins = pe.matmul(out_, stat, mov, start=start, stop=last and p == 2, skip_group_check=True)
                ins.then_inc(unit_used, 1)

            def step(k, i, mid):
                s = S[k]
                for j in range(s.pair):
                    if j % s.units == 0:
                        b = j // s.units
                        pe.wait_ge(bank_free[b], i + (block0[k] // 2 + 1))
                    if k in OPS:
                        pe.wait_ge(op_ready, op0[k] + (j % s.units + 1) * UK)
                    unit(k, i, j)
                    if mid is not None:
                        mid(i, j)

            def run(k, mid=None, begin=0, end=None):
                end = S[k].steps if end is None else end
                if end - begin == 1:
                    step(k, begin, mid)
                    return
                with pe.Fori(begin, end) as i:
                    step(k, i, mid)

            pe.wait_ge(consts, 2)
            pe.wait_ge(bank_free[1], 1)
            pe.wait_ge(gain_mix_in, 16)
            pe.transpose(gp[:, 1, 0, 0:DT], vec_rows[0:DT, 0], ident[0:DT, 0:DT]).then_inc(vec_t, 1)
            for g in range(8):
                if g >= 4:
                    pe.wait_ge(turned_out, g - 3)
                for b in range(TB):
                    if g in (0, 4):
                        pe.wait_ge(x_in[g // 4 * TB + b], 16)
                    for m in (2 * g, 2 * g + 1):
                        ins = pe.transpose(mx[:, g % 4, (m % 2) * T + b * P:(m % 2) * T + (b + 1) * P],
                                           x_tok[:, b, m * P:(m + 1) * P], ident[:])
                ins.then_inc(turned, 1)
            pe.wait_ge(vec_in, 16 * 8)
            pe.wait_ge(vec_ready, 1)
            pe.transpose(gp[:, 1, 0, 0:ROWS0], vec_rows[0:ROWS0, 0], ident[0:ROWS0, 0:ROWS0])
            pe.transpose(gp[:, 1, 1, 0:ROWS1], vec_rows[0:ROWS1, 1], ident[0:ROWS1, 0:ROWS1]).then_inc(vec_t, 1)

            for credit in (prod_done, pv_done, s_done, sv_done):
                pe.sem_inc(credit, 1)

            def spread_x(i, j):
                if j == 6:
                    pe.wait_ge(x_inverse, 1)
                    pe.matmul(mx[:, 2, 0:T], ones[:], scan[:], start=True, stop=True, skip_group_check=True).then_inc(x_spread, 1)
                if j == 6:
                    pe.wait_ge(vec_ready, 2)

            run(QF, mid=spread_x, end=1)
            run(QF, begin=1)
            run(IV)

            def level_products(h, b, buf):
                tb = slice(b * P, (b + 1) * P)
                if b == 0:
                    pe.wait_ge(qk_ready, h + 1)
                pe.wait_ge(p_ready, h * 2 + (b + 1))
                part8 = mx[:, 0:2].rearrange("p a n -> p (a n)")
                pe.matmul(part8[:, 0:P], key_head[buf][:, tb], q_a[:, bass.ds(h, 1), tb].rearrange("p a t -> p (a t)"),
                          start=True, stop=True, skip_group_check=True)
                for l in range(MASKED - 1):
                    pe.matmul(part8[:, (l + 1) * P:(l + 2) * P], decay[buf][:, l, tb], decay[buf][:, l, tb],
                              start=True, stop=True, skip_group_check=True)
                c0 = b * P
                pe.matmul(part8[0:CHUNK, MASKED * P:MASKED * P + CHUNK], decay[buf][:, LEVELS - 2, c0:c0 + CHUNK],
                          decay[buf][:, LEVELS - 2, c0 + CHUNK:c0 + P], start=True, stop=True,
                          skip_group_check=True).then_inc(prod_done, 1)

            def values(h):
                pe.wait_ge(v_ready, h + 1)
                pe.wait_ge(o_copied, h + 1)
                pe.matmul(mx[:, 3, T:2 * T], v_head[:, 0], p_t[:, 0:T], start=True, stop=False, skip_group_check=True)
                pe.matmul(mx[:, 3, T + P:2 * T], v_head[:, 1], p_t[:, T:3 * P], start=False, stop=True,
                          skip_group_check=True).then_inc(pv_done, 1)

            def hgrn(i, j):
                h, u, b = i * 2 + j // 8, j % 8, j // 8
                if u == 1:
                    level_products(h, 0, b)
                if u == 4:
                    level_products(h, 1, b)
                    pe.wait_ge(o_copied, h + 1)
                    pe.matmul(mx[:, 3, 0:P], decay[b][:, LEVELS - 1, 0:P], decay[b][:, LEVELS - 1, P:T], start=True,
                              stop=True, skip_group_check=True).then_inc(prod_done, 1)
                if u == 7:
                    pe.wait_ge(p_ready, h * 2 + 3)
                    pe.wait_ge(cross_copied, h + 1)
                    values(h)

            run(GQK, mid=hgrn)

            def hgrn_end(i, j):
                hgrn(i + 3, j)

            def norms(i, j):
                for r in range(3):
                    if j == 4 * r + 1:
                        pe.wait_ge(sq_ready, r + 1)
                        if r:
                            pe.wait_ge(factors_used, r)
                        for h in range(H):
                            ins = pe.matmul(mx[0:H, 2, 0:T], pick[:, H - 1 - h:2 * H - 1 - h], wide[:, h], start=h == 0,
                                            stop=h == H - 1, skip_group_check=True)
                        ins.then_inc(ms_done, 1)
                    if j == 4 * r + 3:
                        pe.wait_ge(factors_ready, r + 1)
                        for h in range(H):
                            for part_ in (f_hi, f_lo):
                                ins = pe.matmul(mx[:, h // 2, (h % 2) * T:(h % 2 + 1) * T],
                                                ident_r[0:H, h:h + 1].broadcast_to([H, P]), part_[0:H],
                                                start=h % 2 == 0 and part_ is f_hi, stop=h % 2 == 1 and part_ is f_lo,
                                                skip_group_check=True)
                        ins.then_inc(factors_spread, 1)

            def attention(i, j):
                h, u = (i - 2) * 4 + j // 4, j % 4
                if u == 0:
                    if j == 0:
                        pe.wait_ge(qk_normed, 1)
                    pe.wait_ge(hank_in, h * 16 + 16)
                    pe.wait_ge(head_ready, h + (H + 1))
                    pe.wait_ge(exp_done, h + 1)
                    kh = g_a[:, 2, bass.ds(h, 1)].rearrange("p a t -> p (a t)")
                    s_ = mx[:, 0]
                    pe.matmul(s_[:, 0:P], hank[:, 0:P], flip[:], start=True, stop=False, skip_group_check=True)
                    pe.matmul(s_[:, P:2 * P], hank[:, P:T], flip[:], start=False, stop=False, skip_group_check=True)
                    pe.matmul(s_[:, 2 * P:3 * P], hank[:, 0:P], flip[:], start=False, stop=False, skip_group_check=True)
                    pe.matmul(s_[:, 0:P], q_head[:, 0:P], kh[:, 0:P], start=False, stop=True, skip_group_check=True)
                    pe.matmul(s_[:, P:3 * P], q_head[:, P:T], kh, start=False, stop=True,
                              skip_group_check=True).then_inc(s_done, 1)
                if u == 2:
                    pe.wait_ge(pn_ready, h + 1)
                    for c in range(3):
                        ins = pe.transpose(mx[:, 1, c * P:(c + 1) * P], p_n[:, c * P:(c + 1) * P], ident[:])
                    ins.then_inc(pt_done, 1)
                if u == 3:
                    pe.wait_ge(pt_copied, h + 1)
                    values(h + H)

            run(GATES, mid=hgrn_end, end=1)
            run(GATES, mid=norms, begin=1, end=2)
            run(GATES, mid=attention, begin=2)
            run(PROJ_A)
            run(PROJ_B)
            run(OUT)

            def norm_sum(r):
                pe.wait_ge(norm_part, r + 1)
                pe.matmul(mx[:, 2, 0:T], ones[:], total[:], start=True, stop=True, skip_group_check=True).then_inc(ms_done, 1)

            def norm_ffn_sum(i, j):
                if j == 3:
                    norm_sum(0)

            run(FFN_IN, mid=norm_ffn_sum, end=1)
            run(FFN_IN, begin=1)
            run(FFN_OUT)

            def v_first(i, j):
                if j == 3:
                    norm_sum(1)
                    for t in range(TB):
                        ins = pe.matmul(mx[:, 3, t:t + 1], total[:, t * P:(t + 1) * P], ones[:, 0:1], start=True,
                                        stop=True, skip_group_check=True)
                    ins.then_inc(ms_done, 1)
                if j == 6:
                    pe.wait_ge(ws_in, 16)
                    for g in range(G):
                        ins = pe.transpose(mx[:, g // 4, (g % 4) * P:(g % 4 + 1) * P], ws_raw[:, g], ident[:])
                    ins.then_inc(ws_turned, 1)

            run(V_IN, mid=v_first, end=1)
            run(V_IN, begin=1)

            def mix(g, j):
                if j != 4:
                    return
                pe.wait_ge(ws_ready, 1)
                pe.wait_ge(v_one_in, g + 1)
                pe.wait_ge(sv_used, g + 1)
                for c in range(4):
                    for b in range(TB):
                        t0 = (c % 2) * T + b * P
                        ins = pe.matmul(mx[:, c // 2, t0:t0 + P], v_one[:, b, c * P:(c + 1) * P],
                                        ws_t[:, b, bass.ds(g, 1)].rearrange("p a n -> p (a n)"),
                                        start=True, stop=True, skip_group_check=True)
                ins.then_inc(sv_done, 1)

            run(UG_IN, mid=mix)

            def x_turn(i, j):
                g = j - 1
                if not 0 <= g < 8:
                    return
                if g == 0:
                    pe.wait_ge(sv_used, G + 1)
                if g >= 4:
                    pe.wait_ge(fin_copied, g - 3)
                b, c = g // 4, g % 4
                for m in range(4):
                    ins = pe.transpose(mx[:, g % 4, m * P:(m + 1) * P], x_t[:, 4 * c + m, b * P:(b + 1) * P], ident[:])
                ins.then_inc(fin_turned, 1)

            run(Y_OUT, mid=x_turn, end=1)
            run(Y_OUT, begin=1)


def kernel(**inputs):
    import numpy as np
    import concourse.bacc as bacc
    from concourse.bass_utils import run_bass_kernel_spmd

    nc = bacc.Bacc("TRN2", target_bir_lowering=False, num_devices=1)
    arrays = {}

    def given(name):
        a = np.ascontiguousarray(inputs[name])
        arrays[name + "_in"] = a
        return nc.dram_tensor(name + "_in", a.shape, F32, kind="ExternalInput").ap()

    one = lambda name: given(name)[0]
    out = nc.dram_tensor("result", [1, T, D], F32, kind="ExternalOutput").ap()
    build(nc, one("x"), one("w_in"), one("b_gate"), one("norm_mix"), one("norm_ffn"),
          given("hgrn_lb_logits").rearrange("a n -> (a n)"), one("hgrn_out_gain"), one("q_gain"), one("k_gain"),
          one("rel_bias"), one("w_proj_a"), one("w_proj_b"), one("w_out"), one("w_ffn_in"), one("w_ffn_out"),
          one("a_norm_2"), one("a_w_in_2"), one("a_v_gain_2"), one("a_w_s_2"),
          one("a_b_s_2").rearrange("g n -> (g n)"), one("a_w_out_2"), given("final_norm_2"), out[0])
    got = run_bass_kernel_spmd(nc, [arrays], core_ids=[0])
    return got.results[0]["result"]
```
